# Optimizing a Trainium2 kernel written in Bass

```python
import math
import jax, jax.numpy as jnp
from jax import lax
import numpy as np

D_MODEL = 2048
BATCH = 1
SEQ = 256
DEPTH = 1

RET_HEADS = 8
RET_DK = 128
RET_DV = 256
RET_QK = RET_HEADS * RET_DK
RET_V = RET_HEADS * RET_DV
RET_CHUNK = 128
ROPE_BASE = 10000.0
SSD_INNER = 2 * D_MODEL
SSD_HEAD_DIM = 64
SSD_HEADS = SSD_INNER // SSD_HEAD_DIM
SSD_GROUPS = 8
SSD_STATE = 128
SSD_CONV = 4
SSD_CHUNK = 128
SSD_CONV_DIM = SSD_INNER + 2 * SSD_GROUPS * SSD_STATE
MEM_LEN = 256
XA_HEADS = 4
XA_HEAD_DIM = D_MODEL // XA_HEADS
D_FF = 4 * D_MODEL
EPS = 1e-6

IN_SIZES = [RET_QK, RET_QK, RET_V, RET_V, SSD_INNER, SSD_CONV_DIM, SSD_HEADS, D_MODEL, D_MODEL]
IN_WIDTH = sum(IN_SIZES)
IN_SPLIT_IDX = [int(i) for i in np.cumsum(IN_SIZES)[:-1]]

kernel_name = 'hybrid_retention_ssd_gated_block'

def rms_norm(x, w):
    xf = x.astype(jnp.float32)
    y = xf * lax.rsqrt(jnp.mean(xf * xf, axis=-1, keepdims=True) + EPS)
    return (y * w.astype(jnp.float32)).astype(x.dtype)

def rotary(x, pos):
    d = x.shape[-1]
    half = d // 2
    inv = jnp.exp(-math.log(ROPE_BASE) * jnp.arange(half, dtype=jnp.float32) / half)
    ang = pos[:, None] * inv[None, :]
    cos = jnp.cos(ang)[None, :, None, :]
    sin = jnp.sin(ang)[None, :, None, :]
    x1, x2 = x[..., :half], x[..., half:]
    return jnp.concatenate([x1 * cos - x2 * sin, x1 * sin + x2 * cos], axis=-1)

def retention(q, k, v):
    bsz, seq, nh, dk = q.shape
    dv = v.shape[-1]
    c = RET_CHUNK
    nc = seq // c
    log_g = jnp.log(1.0 - jnp.exp2(-5.0 - jnp.arange(nh, dtype=jnp.float32)))
    q = q.reshape(bsz, nc, c, nh, dk)
    k = k.reshape(bsz, nc, c, nh, dk)
    v = v.reshape(bsz, nc, c, nh, dv)
    idx = jnp.arange(c, dtype=jnp.float32)
    rel = idx[:, None] - idx[None, :]
    decay_in = jnp.where(rel[None] >= 0, jnp.exp(jnp.maximum(rel, 0.0)[None] * log_g[:, None, None]), 0.0)
    scores = jnp.einsum('bnihd,bnjhd->bnhij', q, k) * decay_in
    inner = jnp.einsum('bnhij,bnjhe->bnihe', scores, v)
    zeta = jnp.exp((c - 1 - idx)[None, :] * log_g[:, None])
    chunk_kv = jnp.einsum('bnjhd,hj,bnjhe->bnhde', k, zeta, v)
    chunk_decay = jnp.exp(c * log_g)[:, None, None]

    def step(state, kv):
        return chunk_decay * state + kv, state

    init = jnp.zeros((bsz, nh, dk, dv), chunk_kv.dtype)
    _, prev = lax.scan(step, init, jnp.moveaxis(chunk_kv, 1, 0))
    prev = jnp.moveaxis(prev, 0, 1)
    xi = jnp.exp((idx + 1.0)[None, :] * log_g[:, None])
    cross = jnp.einsum('bnihd,bnhde,hi->bnihe', q, prev, xi)
    return (inner + cross).reshape(bsz, seq, nh, dv)

def head_group_norm(y, w):
    bsz, seq = y.shape[:2]
    yf = y.astype(jnp.float32)
    mu = jnp.mean(yf, axis=-1, keepdims=True)
    var = jnp.mean(jnp.square(yf - mu), axis=-1, keepdims=True)
    yn = ((yf - mu) * lax.rsqrt(var + EPS)).reshape(bsz, seq, -1)
    return yn * w.astype(jnp.float32)

def causal_conv(x, w, b):
    ch = x.shape[-1]
    y = lax.conv_general_dilated(x, w[:, None, :].astype(x.dtype), window_strides=(1,),
                                 padding=[(SSD_CONV - 1, 0)],
                                 dimension_numbers=('NWC', 'WIO', 'NWC'),
                                 feature_group_count=ch)
    return y + b

def ssd_scan(x, dt, a, bm, cm):
    bsz, seq, nh, hp = x.shape
    g, n = bm.shape[2], bm.shape[3]
    r = nh // g
    qc = SSD_CHUNK
    nc = seq // qc
    x = x.reshape(bsz, nc, qc, g, r, hp)
    dt = dt.reshape(bsz, nc, qc, g, r)
    bm = bm.reshape(bsz, nc, qc, g, n)
    cm = cm.reshape(bsz, nc, qc, g, n)
    da = dt * a.reshape(g, r)
    a_cs = jnp.cumsum(da, axis=2)
    xdt = x * dt[..., None]
    mask = jnp.tril(jnp.ones((qc, qc), dtype=bool))[None, None, :, :, None, None]
    seg = a_cs[:, :, :, None] - a_cs[:, :, None, :]
    lmat = jnp.exp(jnp.where(mask, seg, -jnp.inf))
    cb = jnp.einsum('bclgn,bcsgn->bclsg', cm, bm)
    y_diag = jnp.einsum('bclsg,bclsgr,bcsgrp->bclgrp', cb, lmat, xdt)
    decay_states = jnp.exp(a_cs[:, :, -1:] - a_cs)
    states = jnp.einsum('bclgn,bclgr,bclgrp->bcgrpn', bm, decay_states, xdt)
    chunk_decay = jnp.exp(a_cs[:, :, -1])[..., None, None]

    def step(s, inp):
        st, dec = inp
        return dec * s + st, s

    init = jnp.zeros((bsz, g, r, hp, n), states.dtype)
    _, prev = lax.scan(step, init, (jnp.moveaxis(states, 1, 0), jnp.moveaxis(chunk_decay, 1, 0)))
    prev = jnp.moveaxis(prev, 0, 1)
    y_off = jnp.einsum('bclgn,bcgrpn,bclgr->bclgrp', cm, prev, jnp.exp(a_cs))
    return (y_diag + y_off).reshape(bsz, seq, nh, hp)

def gated_rms_norm(y, z, w):
    bsz, seq, d = y.shape
    gy = (y * jax.nn.silu(z)).astype(jnp.float32).reshape(bsz, seq, SSD_GROUPS, d // SSD_GROUPS)
    gy = gy * lax.rsqrt(jnp.mean(gy * gy, axis=-1, keepdims=True) + EPS)
    return gy.reshape(bsz, seq, d) * w.astype(jnp.float32)

def setup_inputs(seed: int = 0) -> dict:
    key = jax.random.key(seed)
    ks = iter(jax.random.split(key, 32))
    f32 = jnp.float32

    def nrm(shape, fan_in):
        return jax.random.normal(next(ks), shape, f32) * (fan_in ** -0.5)

    def gain(shape):
        return 1.0 + 0.02 * jax.random.normal(next(ks), shape, f32)

    x = jax.random.normal(next(ks), (BATCH, SEQ, D_MODEL), f32)
    mem = jax.random.normal(next(ks), (BATCH, MEM_LEN, D_MODEL), f32)
    dt0 = jnp.exp(jax.random.uniform(next(ks), (DEPTH, SSD_HEADS), f32, math.log(1e-3), math.log(1e-1)))
    dt_bias = dt0 + jnp.log(-jnp.expm1(-dt0))
    a_log = jnp.log(jax.random.uniform(next(ks), (DEPTH, SSD_HEADS), f32, 1.0, 16.0))
    return {
        'x': x,
        'mem': mem,
        'norm_mix_w': gain((DEPTH, D_MODEL)),
        'w_in': nrm((DEPTH, D_MODEL, IN_WIDTH), D_MODEL),
        'conv_w': nrm((DEPTH, SSD_CONV, SSD_CONV_DIM), SSD_CONV),
        'conv_b': 0.02 * jax.random.normal(next(ks), (DEPTH, SSD_CONV_DIM), f32),
        'dt_bias': dt_bias,
        'a_log': a_log,
        'd_skip': gain((DEPTH, SSD_HEADS)),
        'ret_norm_w': gain((DEPTH, RET_V)),
        'ssd_norm_w': gain((DEPTH, SSD_INNER)),
        'w_ret_out': nrm((DEPTH, RET_V, D_MODEL), RET_V),
        'w_ssd_out': nrm((DEPTH, SSD_INNER, D_MODEL), SSD_INNER),
        'w_mix_out': nrm((DEPTH, D_MODEL, D_MODEL), D_MODEL),
        'norm_xa_w': gain((DEPTH, D_MODEL)),
        'mem_norm_w': gain((DEPTH, D_MODEL)),
        'w_xq': nrm((DEPTH, D_MODEL, D_MODEL), D_MODEL),
        'w_xkv': nrm((DEPTH, D_MODEL, 2 * D_MODEL), D_MODEL),
        'w_xo': nrm((DEPTH, D_MODEL, D_MODEL), D_MODEL),
        'norm_ff_w': gain((DEPTH, D_MODEL)),
        'w_ff1': nrm((DEPTH, D_MODEL, D_FF), D_MODEL),
        'w_ff2': nrm((DEPTH, D_FF, D_MODEL), D_FF),
        'final_norm_w': gain((D_MODEL,)),
    }

def reference(x, mem, norm_mix_w, w_in, conv_w, conv_b, dt_bias, a_log, d_skip, ret_norm_w, ssd_norm_w,
              w_ret_out, w_ssd_out, w_mix_out, norm_xa_w, mem_norm_w, w_xq, w_xkv, w_xo,
              norm_ff_w, w_ff1, w_ff2, final_norm_w):
    bsz, seq, _ = x.shape
    mem_len = mem.shape[1]
    pos = jnp.arange(seq, dtype=jnp.float32)
    h = x
    for l in range(DEPTH):
        xn = rms_norm(h, norm_mix_w[l])
        q, k, v, g_ret, z, xbc, dt_raw, gate_a, gate_b = jnp.split(xn @ w_in[l], IN_SPLIT_IDX, axis=-1)
        q = rotary(q.reshape(bsz, seq, RET_HEADS, RET_DK), pos) * (RET_DK ** -0.5)
        k = rotary(k.reshape(bsz, seq, RET_HEADS, RET_DK), pos)
        v = v.reshape(bsz, seq, RET_HEADS, RET_DV)
        y_ret = head_group_norm(retention(q, k, v), ret_norm_w[l]) * jax.nn.silu(g_ret)
        br_ret = y_ret @ w_ret_out[l]
        xbc = jax.nn.silu(causal_conv(xbc, conv_w[l], conv_b[l]))
        xs, bm, cm = jnp.split(xbc, [SSD_INNER, SSD_INNER + SSD_GROUPS * SSD_STATE], axis=-1)
        dt = jax.nn.softplus(dt_raw.astype(jnp.float32) + dt_bias[l].astype(jnp.float32))
        a = -jnp.exp(a_log[l].astype(jnp.float32))
        xs = xs.reshape(bsz, seq, SSD_HEADS, SSD_HEAD_DIM)
        y_ssd = ssd_scan(xs, dt, a,
                         bm.reshape(bsz, seq, SSD_GROUPS, SSD_STATE),
                         cm.reshape(bsz, seq, SSD_GROUPS, SSD_STATE))
        y_ssd = y_ssd + d_skip[l][:, None] * xs
        y_ssd = gated_rms_norm(y_ssd.reshape(bsz, seq, SSD_INNER), z, ssd_norm_w[l])
        br_ssd = y_ssd @ w_ssd_out[l]
        merged = jax.nn.sigmoid(gate_a) * br_ret + jax.nn.sigmoid(gate_b) * br_ssd
        h = h + (merged @ w_mix_out[l]).astype(h.dtype)
        xn = rms_norm(h, norm_xa_w[l])
        mn = rms_norm(mem, mem_norm_w[l])
        qx = (xn @ w_xq[l]).reshape(bsz, seq, XA_HEADS, XA_HEAD_DIM)
        kx, vx = jnp.split(mn @ w_xkv[l], 2, axis=-1)
        kx = kx.reshape(bsz, mem_len, XA_HEADS, XA_HEAD_DIM)
        vx = vx.reshape(bsz, mem_len, XA_HEADS, XA_HEAD_DIM)
        s = jnp.einsum('bqhd,bmhd->bhqm', qx, kx).astype(jnp.float32) * (XA_HEAD_DIM ** -0.5)
        p = jax.nn.softmax(s, axis=-1).astype(vx.dtype)
        o = jnp.einsum('bhqm,bmhd->bqhd', p, vx).reshape(bsz, seq, D_MODEL)
        h = h + (o @ w_xo[l]).astype(h.dtype)
        xn = rms_norm(h, norm_ff_w[l])
        h = h + (jnp.square(jax.nn.relu(xn @ w_ff1[l])) @ w_ff2[l]).astype(h.dtype)
    return rms_norm(h, final_norm_w)


_drawn_inputs = setup_inputs


def setup_inputs(seed=0):
    import zlib

    import numpy as np

    out = dict(_drawn_inputs(seed))
    spreads = {}
    factors = {'norm_mix_w': 2.881,
     'conv_b': 4.095,
     'd_skip': 171.724,
     'ret_norm_w': 8.0,
     'ssd_norm_w': 5.773,
     'norm_xa_w': 8.0,
     'mem_norm_w': 8.0,
     'norm_ff_w': 11.705,
     'final_norm_w': 22.766}
    for name, (base, spread) in spreads.items():
        noise = np.random.default_rng([zlib.crc32(name.encode()), seed]).standard_normal(out[name].shape)
        drawn = base * np.exp(spread * noise) if base else spread * noise
        out[name] = __import__('jax').numpy.asarray(drawn.astype(out[name].dtype))
    for name, factor in factors.items():
        out[name] = (out[name] * factor).astype(out[name].dtype)
    return out
```

```python
import math
from contextlib import ExitStack

import numpy as np

import concourse.bass as bass
from concourse import mybir

F32 = mybir.dt.float32
F32R = mybir.dt.float32r
ALU = mybir.AluOpType
ACT = mybir.ActivationFunctionType
AX = mybir.AxisListType
ds = bass.ds

P = 128
D = 2048
T = 256
NT = T // P
KT = D // P
EPS = 1e-6
HEADS, DK, DV = 8, 128, 256
INNER, SH, SP_, SG, SN = 4096, 64, 64, 8, 128
RH = SH // SG
CONV = INNER + 2 * SG * SN
XH, XD = 4, 512
FF = 8192
N = 512
CK = 2
RAW, RING, LEAD = 4, 4, 3

Q0, K0, V0 = 0, HEADS * DK, 2 * HEADS * DK
G0 = V0 + HEADS * DV
Z0 = G0 + HEADS * DV
X0 = Z0 + INNER
B0 = X0 + INNER
DT0 = X0 + CONV
GA0 = DT0 + SH
GB0 = GA0 + D

V_MIX, V_XA, V_MEM, V_FF, V_RET, V_SSD, V_CB, V_CW = 0, 16, 32, 48, 64, 80, 112, 160
V_ALL = V_CW + 4 * (CONV // P)

C_ID, C_TRI, C_TGT, C_ONE, C_COS, C_SIN, C_ZETA, C_XI = 0, 128, 256, 384, 512, 640, 768, 776
C_ALL = 784

PHASES = [("qkv", 8, 8), ("gate", 4, 8), ("sig_a", 4, 8), ("ret_out", 4, 8), ("dt", 0, 4), ("bc", 4, 8),
          ("xz", 16, 8), ("sig_b", 4, 8), ("ssd_out", 4, 16), ("mix", 4, 8), ("xv", 4, 8), ("kq", 8, 8),
          ("xo", 4, 8), ("ff1a", 8, 8), ("ff2a", 4, 16), ("ff1b", 8, 8), ("ff2b", 4, 16)]
CHUNK, GROUP = {}, {}
_c = _g = 0
for _n, _k, _s in PHASES:
    CHUNK[_n], GROUP[_n] = _c, _g
    _c += max(_k, 1) * _s
    _g += _k
CPG = {n: s for n, _, s in PHASES}
COUNT = {n: k for n, k, _ in PHASES}
CHUNKS = _c
PACKS, SPLITS = {}, {}
_c = _g = 0
for _n, _k, _s in [("x", 8, 8), ("gate", 8, 8), ("bc", 8, 0), ("xz", 48, 16), ("ssd_out", 8, 8), ("mem", 8, 8),
                   ("mix", 8, 8), ("kq", 24, 8), ("xo", 8, 8), ("ff1a", 16, 16), ("ff1b", 16, 16)]:
    PACKS[_n], SPLITS[_n] = _c, _g
    _c += _k
    _g += _s
AT_RET, AT_SSD, AT_MEM, AT_XA, AT_FF, AT_HID, AT_X = 0, 0, 0, 16, 0, 16, 32


def hybrid_layer(nc, x, mem, w_in, conv_w, conv_b, dt_bias, a_log, d_skip, norm_mix_w, ret_norm_w, ssd_norm_w,
                 w_ret_out, w_ssd_out, w_mix_out, norm_xa_w, mem_norm_w, w_xq, w_xkv, w_xo, norm_ff_w, w_ff1,
                 w_ff2, final_norm_w, consts, decay, merged_dram, out):
    with ExitStack() as ctx:
        def sb(name, shape, dt=F32):
            return ctx.enter_context(nc.sbuf_tensor(name, shape, dt))

        def sem(name):
            return ctx.enter_context(nc.semaphore(name))

        raw = sb("raw", [P, RAW, CK * N])
        w_hi = sb("w_hi", [P, RING, CK * N], F32R)
        w_lo = sb("w_lo", [P, RING, CK * N], F32R)
        acts_hi = sb("acts_hi", [P, 48, T], F32R)
        acts_lo = sb("acts_lo", [P, 48, T], F32R)
        cst = sb("cst", [P, C_ALL])
        vec = sb("vec", [P, V_ALL])
        headrow = sb("headrow", [P, 3, SH])
        dtt = sb("dtt", [P, NT, SH])
        da = sb("da", [P, NT, SH])
        eacs = sb("eacs", [P, SH])
        dstate = sb("dstate", [P, SH])
        small = sb("small", [P, 128])
        reg_a = sb("reg_a", [P, 4096])
        reg_b = sb("reg_b", [P, 4096])
        reg_c = sb("reg_c", [P, 4096])
        nat = sb("nat", [P, NT, N])
        bcg = sb("bcg", [P, 2, T])
        junk = sb("junk", [P, N])

        acc = ctx.enter_context(nc.psum_tensor("acc", [P, 4 * N], F32))
        ptr = ctx.enter_context(nc.psum_tensor("ptr", [P, 2, N], F32))
        pss = ctx.enter_context(nc.psum_tensor("pss", [P, 2, N], F32))

        ident = cst[:, C_ID:C_ID + P]
        tri = cst[:, C_TRI:C_TRI + P]
        tri_gt = cst[:, C_TGT:C_TGT + P]
        ones = cst[:, C_ONE:C_ONE + P]
        cos = cst[:, C_COS:C_COS + P].rearrange("p (t a d) -> p t a d", t=NT, a=1)
        sin = cst[:, C_SIN:C_SIN + P].rearrange("p (t a d) -> p t a d", t=NT, a=1)
        ss_x, rs_x = small[:, 0:2], small[:, 2:4]
        ss_mem, rs_mem = small[:, 4:6], small[:, 6:8]
        ss_xa4, ss_xa, rs_xa = small[:, 8:16], small[:, 16:18], small[:, 18:20]
        ss_ff4, ss_ff, rs_ff = small[:, 20:28], small[:, 28:30], small[:, 30:32]
        ss_out, rs_out = small[:, 32:34], small[:, 34:36]
        ss_g, rs_g = small[:, 36:38], small[:, 38:40]
        mx, nmx, sm, rsm = small[:, 40:42], small[:, 42:44], small[:, 44:46], small[:, 46:48]
        bnst = small[:, 48:60].rearrange("p (t s) -> p t s", t=NT)
        bnag = small[:, 60:64]
        mv = small[:, 64:96]
        rgn = small[:, 96:112]
        dec_t = reg_c[:, 0:1024].rearrange("p (h i) -> p h i", h=HEADS)
        qkv = reg_c[:, 1024:2048].rearrange("p (t n) -> p t n", t=NT)
        rot_a = reg_c[:, 2048:2560].rearrange("p (t a d) -> p t a d", t=NT, a=4)
        rot_b = reg_c[:, 2560:3072].rearrange("p (t a d) -> p t a d", t=NT, a=4)
        rot = reg_c[:, 3072:3584].rearrange("p (t a d) -> p t a d", t=NT, a=4)
        rotm = reg_c[:, 3072:3584].rearrange("p (t a n) -> p t a n", t=NT, a=2)
        q_t, k_t = reg_c[:, 3584:3840], reg_c[:, 3840:4096]
        k_z = reg_a[:, 0:128]
        s_t = reg_a[:, 128:384].rearrange("p (c i) -> p c i", c=NT)
        kv_sb, cross_sb = reg_a[:, 384:640], reg_a[:, 640:896]
        y_ret = reg_b[:, :].rearrange("p (t n) -> p t n", t=NT)
        gated = reg_a[:, 0:1024].rearrange("p (t n) -> p t n", t=NT)
        sig_a = reg_c[:, :].rearrange("p (t n) -> p t n", t=NT)
        merged = sig_a
        bc_t = reg_a[:, :].rearrange("p (j n) -> p j n", j=16)
        conv = reg_b[:, 0:1024].rearrange("p (q n) -> p q n", q=4)
        xdtd, prev = reg_b[:, 0:512], reg_b[:, 512:1024]
        xs_n = reg_b[:, 1024:2048].rearrange("p (t n) -> p t n", t=NT)
        xdt = reg_b[:, 2048:3072].rearrange("p (t n) -> p t n", t=NT)
        y_ssd = reg_b[:, 3072:4096].rearrange("p (t n) -> p t n", t=NT)
        d_tri = reg_c[:, 0:1024]
        e_m = [reg_c[:, 1024:2048], reg_c[:, 2048:3072]]
        s_z = reg_c[:, 3072:4096].rearrange("p (t n) -> p t n", t=NT)
        cbm = nat[:, 0, 0:2 * P].rearrange("p (c l) -> p c l", c=NT)
        bn_sb = nat[:, 0, 2 * P:3 * P]
        hres = reg_a[:, :].rearrange("p (t n) -> p t n", t=NT)
        sig_b = reg_b[:, :].rearrange("p (t n) -> p t n", t=NT)
        mem_n = sig_b
        v_x = reg_c[:, :].rearrange("p (t n) -> p t n", t=NT)
        kx_t = reg_b[:, 0:1024].rearrange("p (q n) -> p q n", q=4)
        qx_t = reg_b[:, 1024:2048].rearrange("p (q n) -> p q n", q=4)
        prob = reg_b[:, 2048:2560].rearrange("p (t n) -> p t n", t=NT)
        prob_t = reg_b[:, 2560:3072]
        o_n = reg_b[:, 3072:4096].rearrange("p (t n) -> p t n", t=NT)
        sq_n = reg_b[:, 0:1024].rearrange("p (t n) -> p t n", t=NT)
        fnw = reg_c[:, 0:2048]

        w_landed = [sem(f"w_landed{s}") for s in range(RAW)]
        hi_ready = sem("hi_ready")
        lo_ready = sem("lo_ready")
        w_used = sem("w_used")
        acc_read = sem("acc_read")
        tp_done = sem("tp_done")
        tp_hi = sem("tp_hi")
        tp_read = sem("tp_read")
        in_x = [sem(f"in_x{j}") for j in range(4)]
        in_cst, in_vec, in_head, in_dec = (sem(n) for n in ("in_cst", "in_vec", "in_head", "in_dec"))
        in_mem, in_h, in_m, in_fn = (sem(n) for n in ("in_mem", "in_h", "in_m", "in_fn"))
        m_stored, out_stored = sem("m_stored"), sem("out_stored")
        vec_turned, vec_ready = sem("vec_turned"), sem("vec_ready")
        ss_done = sem("ss_done")
        var_done = sem("var_done")
        sqrt_done = sem("sqrt_done")
        rs_done = sem("rs_done")
        rotated, kz_ready, qk_turned, qk_copied = (sem(n) for n in ("rotated", "kz_ready", "qk_turned", "qk_copied"))
        scores_done, decayed, kv_copied = (sem(n) for n in ("scores_done", "decayed", "kv_copied"))
        inner_done, cross_copied, y_stored = (sem(n) for n in ("inner_done", "cross_copied", "y_stored"))
        gated_ready = sem("gated_ready")
        dt_1, dt_2, dt_3, dt_4, dt_5 = (sem(f"dt_{j}") for j in range(1, 6))
        da_ready, acs_done, acs_copied, ds_ready, ds_exp = (
            sem(n) for n in ("da_ready", "acs_done", "acs_copied", "ds_ready", "ds_exp"))
        tap_done = sem("tap_done")
        conv_done, bc_ready = sem("conv_done"), sem("bc_ready")
        xconv_done, xs_act, xdt_ready = sem("xconv_done"), sem("xs_act"), sem("xdt_ready")
        bcg_ready, cb_done, bn_ready, cbm_ready = (sem(n) for n in ("bcg_ready", "cb_done", "bn_ready", "cbm_ready"))
        dtri_ready, seg_done, exp_done, mt_ready = (sem(n) for n in ("dtri_ready", "seg_done", "exp_done", "mt_ready"))
        states_done, prev_ready, ydiag_done, yoff_done = (
            sem(n) for n in ("states_done", "prev_ready", "ydiag_done", "yoff_done"))
        y_added, y_gated, gss_done, gvar_done, gsqrt_done, grs_done, y_ready = (
            sem(n) for n in ("y_added", "y_gated", "gss_done", "gvar_done", "gsqrt_done", "grs_done", "y_ready"))
        merged_ready, hg_ready, h_saved = sem("merged_ready"), sem("hg_ready"), sem("h_saved")
        xscores_done, nmx_ready, prob_ready, pt_done, pt_copied, pv_done, o_ready = (
            sem(n) for n in ("xscores_done", "nmx_ready", "prob_ready", "pt_done", "pt_copied", "pv_done", "o_ready"))
        sq_ready, h_done = sem("sq_ready"), sem("h_done")

        def need(eng, s, value):
            if isinstance(value, int) and value <= 0:
                return
            eng.wait_ge(s, value)

        def join(*parts):
            slots = {}
            for part in parts:
                for c, steps in part.items():
                    slots.setdefault(c, []).extend(steps)
            return slots

        def acc_of(i, t):
            if isinstance(i, int):
                return acc[:, (i % 2) * 2 * N + t * N:(i % 2) * 2 * N + (t + 1) * N]
            return acc[:, ds((i % 2) * (2 * N) + t * N, N)]

        def acc_both(i):
            if isinstance(i, int):
                a = acc[:, (i % 2) * 2 * N:(i % 2 + 1) * 2 * N]
            else:
                a = acc[:, ds((i % 2) * (2 * N), 2 * N)]
            return a.rearrange("p (t n) -> p t n", t=NT)

        def group_end(phase, i):
            return CHUNK[phase] + CPG[phase] * (i + 1)

        def landed(phase, slot, uses):
            if phase == "qkv":
                return 48 * uses
            return 32 * uses + 16 * (COUNT["qkv"] * CPG["qkv"] // RAW + (slot < LEAD))

        def tile_rows(w):
            return w.rearrange("(k p) n -> p k n", p=P)

        block = ctx.enter_context(nc.Block())

        @block.sync
        def _(sp):
            xv = x.rearrange("b (t p) n -> p (b t) n", p=P)
            for j in range(4):
                sp.dma_start(hres[:, :, j * N:(j + 1) * N], xv[:, :, j * N:(j + 1) * N]).then_inc(in_x[j], 16)

            def bring(n, c, parts):
                need(sp, lo_ready, n - RAW + 1)
                for dst, src in parts:
                    sp.dma_start(dst, src).then_inc(w_landed[c % RAW], 16)

            def plain(phase, w, col, i, k_base=0, first=0):
                wv = tile_rows(w)
                for c in range(first, CPG[phase]):
                    dst = raw[:, c % RAW, :].rearrange("p (k n) -> p k n", k=CK)
                    bring(CHUNK[phase] + CPG[phase] * i + c, c,
                          [(dst[:, k, :], wv[:, k_base + c * CK + k, col]) for k in range(CK)])

            wi = tile_rows(w_in[0])

            def heads_qkv(i):
                for c in range(CPG["qkv"]):
                    dst = raw[:, c % RAW, :].rearrange("p (k n) -> p k n", k=CK)
                    kk = slice(c * CK, c * CK + CK)
                    qk = wi[:, kk, 0:2 * HEADS * DK].rearrange("p k (a n) -> p k a n", a=2)
                    need(sp, lo_ready, CHUNK["qkv"] + CPG["qkv"] * i + c - RAW + 1)
                    sp.dma_start(dst[:, :, 2 * DK:], wi[:, kk, ds(i * DV + V0, DV)]).then_inc(w_landed[c % RAW], 16)
                    for k in range(CK):
                        sp.dma_start(dst[:, k, 0:2 * DK].rearrange("p (a n) -> p a n", a=2),
                                     qk[:, k, :, ds(i * DK, DK)]).then_inc(w_landed[c % RAW], 16)

            heads_qkv(0)
            with sp.Fori(1, HEADS) as i:
                heads_qkv(i)
            for c in range(LEAD):
                dst = raw[:, c % RAW, :].rearrange("p (k n) -> p k n", k=CK)
                bring(CHUNK["gate"] + c, c, [(dst[:, 0, 0:N // 2], wi[:, CK * c, G0:G0 + N // 2]),
                                             (dst[:, 0, N // 2:], wi[:, CK * c, G0 + N // 2:G0 + N]),
                                             (dst[:, 1, :], wi[:, CK * c + 1, G0:G0 + N])])
            plain("gate", w_in[0], slice(G0, G0 + N), 0, first=LEAD)
            with sp.Fori(1, 4) as i:
                plain("gate", w_in[0], ds(i * N + G0, N), i)
            with sp.Fori(0, 4) as i:
                plain("sig_a", w_in[0], ds(i * N + GA0, N), i)
            with sp.Fori(0, 4) as i:
                plain("ret_out", w_ret_out[0], ds(i * N, N), i)
            for c in range(CPG["dt"]):
                dst = raw[:, c % RAW, 0:4 * SH].rearrange("p (k n) -> p k n", k=4)
                bring(CHUNK["dt"] + c, c, [(dst[:, 2 * k:2 * k + 2, :], wi[:, 4 * c + 2 * k:4 * c + 2 * k + 2,
                                                                          DT0:DT0 + SH]) for k in range(2)])
            with sp.Fori(0, 4) as i:
                plain("bc", w_in[0], ds(i * N + B0, N), i)
            with sp.Fori(0, SG) as g:
                plain("xz", w_in[0], ds(g * N + X0, N), g * 2)
                plain("xz", w_in[0], ds(g * N + Z0, N), g * 2 + 1)
            with sp.Fori(0, 4) as i:
                plain("sig_b", w_in[0], ds(i * N + GB0, N), i)
            with sp.Fori(0, 4) as i:
                plain("ssd_out", w_ssd_out[0], ds(i * N, N), i)
            with sp.Fori(0, 4) as i:
                plain("mix", w_mix_out[0], ds(i * N, N), i)
            with sp.Fori(0, 4) as i:
                plain("xv", w_xkv[0], ds(i * N + D, N), i)
            with sp.Fori(0, XH) as i:
                plain("kq", w_xkv[0], ds(i * N, N), i * 2)
                plain("kq", w_xq[0], ds(i * N, N), i * 2 + 1)
            with sp.Fori(0, 4) as i:
                plain("xo", w_xo[0], ds(i * N, N), i)
            for half, (up, down) in enumerate((("ff1a", "ff2a"), ("ff1b", "ff2b"))):
                with sp.Fori(0, 8) as i:
                    plain(up, w_ff1[0], ds(i * N + half * (FF // 2), N), i)
                with sp.Fori(0, 4) as i:
                    plain(down, w_ff2[0], ds(i * N, N), i, k_base=half * (FF // 2 // P))
            ov = out.rearrange("b (t p) n -> p (b t) n", p=P)
            for t in range(NT):
                sp.wait_ge(h_done, t + 1)
                sp.dma_start(ov[:, t, :], hres[:, t, :]).then_inc(out_stored, 16)
            sp.wait_ge(out_stored, 16 * NT)

        @block.gpsimd
        def _(pool):
            for j, w in enumerate((dt_bias, a_log, d_skip)):
                pool.dma_start(headrow[:, j, :], w.partition_broadcast(P)[:, 0, :]).then_inc(in_head, 16)
            pool.dma_start(dec_t, decay.rearrange("p (h i) -> p h i", h=HEADS)).then_inc(in_dec, 16)
            pool.wait_ge(acc_read, GROUP["ret_out"] + 4)
            pool.dma_start(merged_dram.rearrange("p (t n) -> p t n", t=NT), merged).then_inc(m_stored, 16)
            pool.wait_ge(bc_ready, 4)
            with pool.Fori(0, SG) as g:
                need(pool, yoff_done, g)
                pool.tensor_copy(bcg[:, 0, :], bc_t[:, ds(g, 1), :].rearrange("p a n -> p (a n)"))
                pool.tensor_copy(bcg[:, 1, :], bc_t[:, ds(g + SG, 1), :].rearrange("p a n -> p (a n)")) \
                    .then_inc(bcg_ready, 1)
            pool.wait_ge(tp_read, PACKS["xz"] + 48)
            pool.wait_ge(m_stored, 16)
            xv = x.rearrange("b (t p) n -> p (b t) n", p=P)
            pool.dma_start(merged, merged_dram.rearrange("p (t n) -> p t n", t=NT)).then_inc(in_m, 16)
            pool.dma_start(hres, xv).then_inc(in_h, 16)
            pool.wait_ge(merged_ready, 4)
            pool.dma_start(mem_n, mem.rearrange("b (t p) n -> p (b t) n", p=P)).then_inc(in_mem, 16)
            pool.wait_ge(pv_done, XH)
            pool.dma_start(fnw, final_norm_w.partition_broadcast(P)).then_inc(in_fn, 16)

        @block.tensor
        def _(pe):
            def turn(dst, src):
                return pe.transpose(dst, src, ident)

            def pack_start(m):
                need(pe, tp_read, m - 1)

            def split_pack(m, b, cols):
                pack_start(m)
                for k in range(2):
                    for t in range(NT):
                        last = turn(ptr[:, b, k * T + t * P:k * T + (t + 1) * P], cols(k, t))
                last.then_inc(tp_done, 1)

            def gemm(phase, i, at, hooks, parity=None, ready=None, lhs_at=0):
                par = i if parity is None else parity
                n0 = CHUNK[phase] + CPG[phase] * i
                need(pe, acc_read, GROUP[phase] + i - 1)
                for c in range(CPG[phase]):
                    if ready and c in ready:
                        pe.wait_ge(tp_read, ready[c])
                    need(pe, lo_ready, n0 + c + 1)
                    for k in range(CK):
                        kt = c * CK + k
                        for t in range(NT):
                            xh = acts_hi[:, at + kt, t * P:(t + 1) * P]
                            xl = acts_lo[:, at + kt, t * P:(t + 1) * P]
                            wh = w_hi[:, c % RING, k * N:(k + 1) * N]
                            wl = w_lo[:, c % RING, k * N:(k + 1) * N]
                            o = acc_of(par, t)
                            pe.matmul(o, xh, wh, start=kt == 0, stop=False)
                            pe.matmul(o, xh, wl, start=False, stop=False)
                            last = pe.matmul(o, xl, wh, start=False, stop=kt == CPG[phase] * CK - 1)
                    last.then_inc(w_used, 1)
                    for step in hooks.get(c, ()):
                        step()

            pe.wait_ge(in_cst, 16)
            pe.wait_ge(in_vec, 144)
            stage = reg_b[:, 2048:2048 + 4 * P].rearrange("p (j n) -> p j n", j=4)
            for j, (r, v) in enumerate(((112, 0), (48, V_CB), (96, V_CW), (96, V_CW + 96))):
                last = pe.transpose(pss[:, 0, v:v + r], stage[0:r, j, :], ident[0:r, 0:r])
            last.then_inc(vec_turned, 1)
            for m in range(8):
                if m % 2 == 0:
                    pe.wait_ge(in_x[m // 2], 16)
                split_pack(PACKS["x"] + m, m % 2, lambda k, t: hres[:, t, (2 * m + k) * P:(2 * m + k + 1) * P])

            def qk_turn(i):
                pe.wait_ge(rotated, i + 1)
                need(pe, qk_copied, i)
                if isinstance(i, int) and i == 0:
                    pe.wait_ge(vec_ready, 1)
                for a in range(2):
                    for t in range(NT):
                        last = turn(pss[:, 0, a * T + t * P:a * T + (t + 1) * P], rotm[:, t, a, :])
                last.then_inc(qk_turned, 1)

            def ret_scores(i):
                pe.wait_ge(qk_copied, i + 1)
                pe.wait_ge(kz_ready, i + 1)
                need(pe, decayed, i)
                need(pe, kv_copied, i)
                for c in range(NT):
                    pe.matmul(pss[:, 1, c * P:(c + 1) * P], k_t[:, c * P:(c + 1) * P], q_t[:, c * P:(c + 1) * P],
                              start=True, stop=True)
                pe.matmul(pss[:, 1, T:T + DV], k_z, qkv[:, 0, 2 * DK:], start=True, stop=True) \
                    .then_inc(scores_done, 1)

            def ret_inner(i):
                pe.wait_ge(decayed, i + 1)
                pe.wait_ge(kv_copied, i + 1)
                need(pe, y_stored, i)
                for c in range(NT):
                    pe.matmul(ptr[:, 0, c * DV:(c + 1) * DV], s_t[:, c, :], qkv[:, c, 2 * DK:],
                              start=True, stop=True)
                pe.matmul(ptr[:, 1, 0:DV], q_t[:, P:2 * P], kv_sb, start=True, stop=True).then_inc(inner_done, 1)

            def retention(i):
                return {1: [lambda: qk_turn(i)], 3: [lambda: ret_scores(i)], 5: [lambda: ret_inner(i)]}

            gemm("qkv", 0, AT_X, {}, ready={c: PACKS["x"] + c + 1 for c in range(8)})
            with pe.Fori(1, HEADS) as i:
                gemm("qkv", i, AT_X, retention(i - 1))

            def gate_packs(i):
                pe.wait_ge(gated_ready, i + 1)
                for j in range(2):
                    split_pack(PACKS["gate"] + 2 * i + j, j,
                               lambda k, t: gated[:, t, (2 * j + k) * P:(2 * j + k + 1) * P])

            def gate(i):
                return {2: [lambda: gate_packs(i)]}

            gemm("gate", 0, AT_X, retention(HEADS - 1))
            with pe.Fori(1, 4) as i:
                gemm("gate", i, AT_X, gate(i - 1))
            gemm("sig_a", 0, AT_X, gate(3))
            with pe.Fori(1, 4) as i:
                gemm("sig_a", i, AT_X, {})
            gemm("ret_out", 0, AT_RET, {}, ready={0: PACKS["gate"] + 8})
            with pe.Fori(1, 4) as i:
                gemm("ret_out", i, AT_RET, {})

            for c in range(CPG["dt"]):
                pe.wait_ge(lo_ready, CHUNK["dt"] + c + 1)
                for k in range(4):
                    kt = c * 4 + k
                    for t in range(NT):
                        xh = acts_hi[:, AT_X + kt, t * P:(t + 1) * P]
                        xl = acts_lo[:, AT_X + kt, t * P:(t + 1) * P]
                        wh = w_hi[:, c % RING, k * SH:(k + 1) * SH]
                        wl = w_lo[:, c % RING, k * SH:(k + 1) * SH]
                        o = pss[:, t, 0:SH]
                        pe.matmul(o, xh, wh, start=kt == 0, stop=False)
                        pe.matmul(o, xh, wl, start=False, stop=False)
                        last = pe.matmul(o, xl, wh, start=False, stop=kt == KT - 1)
                last.then_inc(w_used, 1)

            def dt_sums():
                pe.wait_ge(da_ready, 1)
                for t in range(NT):
                    pe.matmul(pss[:, 0, t * SH:(t + 1) * SH], tri, da[:, t, :], start=True, stop=True)
                pe.matmul(pss[:, 0, 2 * SH:3 * SH], ones, da[:, 0, :], start=True, stop=True).then_inc(acs_done, 1)

            def nat_packs(m):
                for j in range(2):
                    split_pack(m + j, j, lambda k, t: nat[:, t, (2 * j + k) * P:(2 * j + k + 1) * P])

            def bc_turn(i):
                pe.wait_ge(acc_read, GROUP["bc"] + i + 1)
                nat_packs(PACKS["bc"] + 2 * i)

            gemm("bc", 0, AT_X, {6: [dt_sums]})
            with pe.Fori(1, 4) as i:
                gemm("bc", i, AT_X, {1: [lambda: bc_turn(i - 1)]})

            def xs_turn(g):
                pe.wait_ge(acc_read, GROUP["xz"] + 2 * g + 1)
                nat_packs(PACKS["xz"] + 6 * g)

            def xs_back(g):
                pe.wait_ge(xs_act, g + 1)
                for t in range(NT):
                    pack_start(PACKS["xz"] + 6 * g + 2 + t)
                    for q in range(4):
                        last = turn(ptr[:, t, q * P:(q + 1) * P], conv[:, q, t * P:(t + 1) * P])
                    last.then_inc(tp_done, 1)

            def ssd_cb(g):
                pe.wait_ge(bcg_ready, g + 1)
                pe.wait_ge(tp_read, PACKS["xz"] + 6 * g + 4)
                turn(ptr[:, 0, 0:P], bcg[:, 0, 0:P])
                for c in range(NT):
                    last = pe.matmul(ptr[:, 0, (c + 1) * P:(c + 2) * P], bcg[:, 0, c * P:(c + 1) * P],
                                     bcg[:, 1, c * P:(c + 1) * P], start=True, stop=True)
                last.then_inc(cb_done, 1)

            def ssd_seg(g, c):
                pe.wait_ge(dtri_ready, 2 * g + c + 1)
                if c == 0:
                    need(pe, exp_done, 2 * g)
                else:
                    pe.wait_ge(exp_done, 2 * g + 1)
                for h in range(2):
                    last = pe.matmul(pss[:, h, :], tri_gt, d_tri[:, h * N:(h + 1) * N], start=True, stop=True)
                last.then_inc(seg_done, 1)

            def ssd_states(g):
                pe.wait_ge(bn_ready, g + 1)
                pe.wait_ge(xdt_ready, g + 1)
                pe.matmul(ptr[:, 1, :], bn_sb, xdtd, start=True, stop=True).then_inc(states_done, 1)

            def ssd_diag(g, c):
                pe.wait_ge(mt_ready, 2 * g + c + 1)
                if c == 0:
                    pe.wait_ge(cbm_ready, g + 1)
                else:
                    pe.wait_ge(y_added, 3 * g + 1)
                for r in range(RH):
                    last = pe.matmul(ptr[:, 0, r * SP_:(r + 1) * SP_], e_m[c][:, r * P:(r + 1) * P],
                                     xdt[:, c, r * SP_:(r + 1) * SP_], start=True, stop=True)
                last.then_inc(ydiag_done, 1)

            def ssd_off(g):
                pe.wait_ge(prev_ready, g + 1)
                pe.matmul(ptr[:, 1, :], bcg[:, 1, P:2 * P], prev, start=True, stop=True).then_inc(yoff_done, 1)

            def ssd_packs(g):
                pe.wait_ge(y_ready, g + 1)
                for j in range(2):
                    split_pack(PACKS["xz"] + 6 * g + 4 + j, j,
                               lambda k, t: y_ssd[:, t, (2 * j + k) * P:(2 * j + k + 1) * P])

            def during_z(g):
                return {3: [lambda: xs_turn(g)], 7: [lambda: xs_back(g)]}

            def during_xs(g):
                return {0: [lambda: ssd_seg(g, 0)], 1: [lambda: ssd_cb(g)], 2: [lambda: ssd_states(g)],
                        3: [lambda: ssd_seg(g, 1)], 4: [lambda: ssd_off(g), lambda: ssd_diag(g, 0)],
                        6: [lambda: ssd_diag(g, 1)]}

            gemm("xz", 0, AT_X, {1: [lambda: bc_turn(3)]}, parity=0)
            gemm("xz", 1, AT_X, during_z(0), parity=1)
            with pe.Fori(1, SG) as g:
                gemm("xz", g * 2, AT_X, during_xs(g - 1), parity=0)
                gemm("xz", g * 2 + 1, AT_X, join({1: [lambda: ssd_packs(g - 1)]}, during_z(g)), parity=1)

            gemm("sig_b", 0, AT_X, during_xs(SG - 1))
            gemm("sig_b", 1, AT_X, {1: [lambda: ssd_packs(SG - 1)]})
            with pe.Fori(2, 4) as i:
                gemm("sig_b", i, AT_X, {})

            def merge_turn(i):
                pe.wait_ge(merged_ready, i + 1)
                nat_packs(PACKS["ssd_out"] + 2 * i)

            gemm("ssd_out", 0, AT_SSD, {}, ready={0: PACKS["xz"] + 48})
            with pe.Fori(1, 4) as i:
                gemm("ssd_out", i, AT_SSD, {2: [lambda: merge_turn(i - 1)]})

            def mem_packs(lo, hi):
                for m in range(lo, hi):
                    if m == 0:
                        pe.wait_ge(in_mem, 16)
                    split_pack(PACKS["mem"] + m, m % 2,
                               lambda k, t: mem_n[:, t, (2 * m + k) * P:(2 * m + k + 1) * P])

            def h_turn(phase, base, i):
                pe.wait_ge(hg_ready, base + i + 1)
                nat_packs(PACKS[phase] + 2 * i)

            gemm("mix", 0, AT_X, {1: [lambda: merge_turn(3)], 4: [lambda: mem_packs(0, 2)],
                                  5: [lambda: mem_packs(2, 4)], 6: [lambda: mem_packs(4, 6)],
                                  7: [lambda: mem_packs(6, 8)]},
                 ready={0: PACKS["ssd_out"] + 6, 6: PACKS["ssd_out"] + 8})
            with pe.Fori(1, 4) as i:
                gemm("mix", i, AT_X, {1: [lambda: h_turn("mix", 0, i - 1)]})

            gemm("xv", 0, AT_MEM, {1: [lambda: h_turn("mix", 0, 3)]})
            with pe.Fori(1, 4) as i:
                gemm("xv", i, AT_MEM, {})

            def k_turn(n):
                pe.wait_ge(acc_read, GROUP["kq"] + 2 * n + 1)
                nat_packs(PACKS["kq"] + 6 * n)

            def q_turn(n):
                pe.wait_ge(acc_read, GROUP["kq"] + 2 * n + 2)
                nat_packs(PACKS["kq"] + 6 * n + 2)

            def x_scores(n):
                pe.wait_ge(tp_read, PACKS["kq"] + 6 * n + 4)
                for t in range(NT):
                    for q in range(4):
                        last = pe.matmul(pss[:, 0, t * T:(t + 1) * T], qx_t[:, q, t * P:(t + 1) * P],
                                         kx_t[:, q, :], start=q == 0, stop=q == 3)
                last.then_inc(xscores_done, 1)

            def p_turn(n):
                pe.wait_ge(prob_ready, n + 1)
                for m in range(NT):
                    for t in range(NT):
                        last = turn(pss[:, 1, m * T + t * P:m * T + (t + 1) * P], prob[:, t, m * P:(m + 1) * P])
                last.then_inc(pt_done, 1)

            def p_v(n):
                pe.wait_ge(pt_copied, n + 1)
                for t in range(NT):
                    for m in range(NT):
                        v = v_x[:, m, n * N:(n + 1) * N] if isinstance(n, int) else v_x[:, m, ds(n * N, N)]
                        last = pe.matmul(pss[:, t, :], prob_t[:, m * T + t * P:m * T + (t + 1) * P], v,
                                         start=m == 0, stop=m == 1)
                last.then_inc(pv_done, 1)

            def o_packs(n):
                pe.wait_ge(o_ready, n + 1)
                for j in range(2):
                    split_pack(PACKS["kq"] + 6 * n + 4 + j, j,
                               lambda k, t: o_n[:, t, (2 * j + k) * P:(2 * j + k + 1) * P])

            def attention(n):
                return {0: [lambda: q_turn(n)], 1: [lambda: x_scores(n)], 2: [lambda: p_turn(n)],
                        3: [lambda: p_v(n)], 4: [lambda: o_packs(n)]}

            gemm("kq", 0, AT_MEM, {}, parity=0)
            gemm("kq", 1, AT_XA, {1: [lambda: k_turn(0)]}, parity=1, ready={0: PACKS["mix"] + 8})
            with pe.Fori(1, XH) as n:
                gemm("kq", n * 2, AT_MEM, attention(n - 1), parity=0)
                gemm("kq", n * 2 + 1, AT_XA, {1: [lambda: k_turn(n)]}, parity=1)
            gemm("xo", 0, AT_X, attention(XH - 1),
                 ready={0: PACKS["kq"] + 18, 6: PACKS["kq"] + 24})
            with pe.Fori(1, 4) as i:
                gemm("xo", i, AT_X, {1: [lambda: h_turn("xo", 4, i - 1)]})

            def sq_turn(phase, i):
                b = 8 if phase == "ff1b" else 0
                pe.wait_ge(sq_ready, b + i + 1)
                for j in range(2):
                    split_pack(PACKS[phase] + 2 * i + j, j,
                               lambda k, t: sq_n[:, t, (2 * j + k) * P:(2 * j + k + 1) * P])

            for up, down in (("ff1a", "ff2a"), ("ff1b", "ff2b")):
                if up == "ff1a":
                    gemm(up, 0, AT_FF, {1: [lambda: h_turn("xo", 4, 3)]},
                         ready={0: PACKS["xo"] + 6, 6: PACKS["xo"] + 8})
                else:
                    gemm(up, 0, AT_FF, {})
                with pe.Fori(1, 8) as i:
                    gemm(up, i, AT_FF, {1: [lambda: sq_turn(up, i - 1)]})
                gemm(down, 0, AT_HID, {1: [lambda: sq_turn(up, 7)]},
                     ready={0: PACKS[up] + 14, 14: PACKS[up] + 16})
                with pe.Fori(1, 4) as i:
                    gemm(down, i, AT_HID, {})

        @block.scalar
        def _(act):
            def copy(o, i, scale=1.0):
                return act.activation(o, i, ACT.Copy, scale=scale)

            def split_hi(phase, i, c):
                n = CHUNK[phase] + CPG[phase] * i + c + LEAD
                s = (c + LEAD) % RAW
                uses = CHUNK[phase] // RAW + (CPG[phase] // RAW) * i + (c + LEAD) // RAW + 1
                act.wait_ge(w_landed[s], landed(phase, s, uses))
                need(act, w_used, n - RING + 1)
                copy(w_hi[:, s, :], raw[:, s, :]).then_inc(hi_ready, 1)

            def slots(phase, i, hooks, final=False):
                for c in range(CPG[phase]):
                    if not (final and c + LEAD >= CPG[phase]):
                        split_hi(phase, i, c)
                    for step in hooks.get(c, ()):
                        step()

            def group_ready(phase, i):
                act.wait_ge(w_used, group_end(phase, i))
                need(act, acc_read, GROUP[phase] + i)

            def hi_pack(phase, m, b, at, col=None, sp_=None):
                act.wait_ge(tp_done, PACKS[phase] + m + 1)
                if col is None:
                    o = acts_hi[:, at:at + 2, :] if isinstance(at, int) else acts_hi[:, ds(at, 2), :]
                    copy(o, ptr[:, b, :].rearrange("p (k n) -> p k n", k=2)).then_inc(tp_hi, 1)
                    return
                for k in range(2):
                    a, v = at + k, col + k
                    o = acts_hi[:, a, :] if isinstance(a, int) else \
                        acts_hi[:, ds(a, 1), :].rearrange("p a n -> p (a n)")
                    sc = vec[:, v:v + 1] if isinstance(v, int) else vec[:, ds(v, 1)]
                    last = copy(o, ptr[:, b, k * T:(k + 1) * T], sc)
                last.then_inc(tp_hi, 1)

            act.dma_start(cst[:], consts).then_inc(in_cst, 16)
            stage = reg_b[:, 2048:2048 + 4 * P].rearrange("p (j n) -> p j n", j=4)
            for v, w in ((V_MIX, norm_mix_w), (V_XA, norm_xa_w), (V_MEM, mem_norm_w), (V_FF, norm_ff_w),
                         (V_RET, ret_norm_w), (V_SSD, ssd_norm_w)):
                n = w.shape[1] // P
                act.dma_start(stage[v:v + n, 0, :], w[0].rearrange("(j p) -> j p", p=P)).then_inc(in_vec, 16)
            act.dma_start(stage[0:48, 1, :], conv_b[0].rearrange("(j p) -> j p", p=P)).then_inc(in_vec, 16)
            cw = conv_w[0].rearrange("k (j p) -> (k j) p", p=P)
            for h in range(2):
                act.dma_start(stage[0:96, 2 + h, :], cw[96 * h:96 * h + 96, :]).then_inc(in_vec, 16)

            for n in range(LEAD):
                act.wait_ge(w_landed[n], landed("qkv", n, 1))
                copy(w_hi[:, n, :], raw[:, n, :]).then_inc(hi_ready, 1)
            act.wait_ge(vec_ready, 1)
            for m in range(8):
                hi_pack("x", m, m % 2, AT_X + 2 * m, V_MIX + 2 * m)
            for t in range(NT):
                last = act.activation(reg_b[:, 0:D], hres[:, t, :], ACT.Square, accum_out=ss_x[:, t:t + 1])
                if t == 0:
                    act.drain()
            last.then_inc(ss_done, 1)

            def root(n, v):
                act.wait_ge(var_done, n)
                act.activation(v, v, ACT.Sqrt).then_inc(sqrt_done, 1)

            def qkv_copy(i):
                group_ready("qkv", i)
                need(act, inner_done, i)
                need(act, rotated, i)
                if isinstance(i, int) and i == 0:
                    act.wait_ge(rs_done, 1)
                for t in range(NT):
                    last = copy(qkv[:, t, :], acc_of(i, t), rs_x[:, t:t + 1])
                last.then_inc(acc_read, 1)

            def qk_copy(i):
                act.wait_ge(qk_turned, i + 1)
                copy(q_t, pss[:, 0, 0:T], DK ** -0.5)
                copy(k_t, pss[:, 0, T:2 * T]).then_inc(qk_copied, 1)

            def kv_copy(i):
                act.wait_ge(scores_done, i + 1)
                act.wait_ge(decayed, i + 1)
                copy(kv_sb, pss[:, 1, T:T + DV]).then_inc(kv_copied, 1)

            def cross_copy(i):
                act.wait_ge(inner_done, i + 1)
                need(act, y_stored, i)
                xi = cst[:, C_XI + i:C_XI + i + 1] if isinstance(i, int) else cst[:, ds(i + C_XI, 1)]
                copy(cross_sb, ptr[:, 1, 0:DV], xi).then_inc(cross_copied, 1)

            def retention(i):
                return {0: [lambda: qkv_copy(i)], 2: [lambda: qk_copy(i)], 4: [lambda: kv_copy(i)],
                        6: [lambda: cross_copy(i)]}

            slots("qkv", 0, {0: [lambda: root(1, rs_x)]})
            with act.Fori(1, HEADS) as i:
                slots("qkv", i, retention(i - 1))

            def gate_silu(i):
                group_ready("gate", i)
                need(act, tp_done, PACKS["gate"] + 2 * i)
                for t in range(NT):
                    last = act.activation(gated[:, t, :], acc_of(i, t), ACT.Silu, scale=rs_x[:, t:t + 1])
                last.then_inc(acc_read, 1)

            def gate_hi(i):
                for j in range(2):
                    hi_pack("gate", 2 * i + j, j, 4 * i + (AT_RET + 2 * j), 4 * i + (V_RET + 2 * j))

            def gate(i):
                return {0: [lambda: gate_silu(i)], 3: [lambda: gate_hi(i)]}

            slots("gate", 0, {**retention(HEADS - 1), 7: [lambda: root(2, rgn)]})
            with act.Fori(1, 4) as i:
                slots("gate", i, gate(i - 1))

            def sig_to(phase, i, dst):
                group_ready(phase, i)
                for t in range(NT):
                    o = dst[:, t, i * N:(i + 1) * N] if isinstance(i, int) else dst[:, t, ds(i * N, N)]
                    last = act.activation(o, acc_of(i, t), ACT.Sigmoid, scale=rs_x[:, t:t + 1])
                last.then_inc(acc_read, 1)

            slots("sig_a", 0, gate(3))
            with act.Fori(1, 4) as i:
                slots("sig_a", i, {1: [lambda: sig_to("sig_a", i - 1, sig_a)]})
            slots("ret_out", 0, {1: [lambda: sig_to("sig_a", 3, sig_a)]})
            with act.Fori(1, 4) as i:
                slots("ret_out", i, {})
            slots("dt", 0, {})

            wk = junk[:, :].rearrange("p (a t n) -> p a t n", a=4, t=NT)

            def dt_exp():
                act.wait_ge(dt_1, 1)
                act.activation(wk[:, 1], wk[:, 1], ACT.Exp).then_inc(dt_2, 1)
                act.activation(headrow[:, 1, :], headrow[:, 1, :], ACT.Exp).then_inc(dt_2, 1)

            def dt_ln():
                act.wait_ge(dt_3, 1)
                act.activation(wk[:, 3], wk[:, 2], ACT.Ln).then_inc(dt_4, 1)

            def acs_copy():
                act.wait_ge(acs_done, 1)
                copy(junk[:, 0:3 * SH], pss[:, 0, 0:3 * SH])
                act.activation(eacs[:, :], pss[:, 0, SH:2 * SH], ACT.Exp).then_inc(acs_copied, 1)

            def ds_exp_():
                act.wait_ge(ds_ready, 1)
                act.activation(dstate[:, :], dstate[:, :], ACT.Exp).then_inc(ds_exp, 1)

            def nat_copy(phase, i, m, scale, parity=None):
                group_ready(phase, i)
                need(act, tp_done, m)
                for t in range(NT):
                    last = copy(nat[:, t, :], acc_of(i if parity is None else parity, t), scale[:, t:t + 1])
                last.then_inc(acc_read, 1)

            def conv_tap(phase, m, b, q0, ct):
                act.wait_ge(tp_done, PACKS[phase] + m + 1)
                for k in range(2):
                    w, v = ct + (V_CW + 3 * (CONV // P) + k), ct + (V_CB + k)
                    w = vec[:, w:w + 1] if isinstance(w, int) else vec[:, ds(w, 1)]
                    v = vec[:, v:v + 1] if isinstance(v, int) else vec[:, ds(v, 1)]
                    last = act.activation(conv[:, q0 + k, :], ptr[:, b, k * T:(k + 1) * T], ACT.Identity,
                                          bias=v, scale=w)
                last.then_inc(tap_done, 1)

            def bc_taps(i):
                for j in range(2):
                    conv_tap("bc", 2 * i + j, j, 2 * j, i * 4 + (INNER // P + 2 * j))

            def bc_silu(i):
                act.wait_ge(conv_done, i + 1)
                o = bc_t[:, 4 * i:4 * i + 4, :] if isinstance(i, int) else bc_t[:, ds(i * 4, 4), :]
                act.activation(o, conv, ACT.Silu).then_inc(bc_ready, 1)

            def bc(i):
                return {0: [lambda: nat_copy("bc", i, PACKS["bc"] + 2 * i, rs_x)], 3: [lambda: bc_taps(i)],
                        7: [lambda: bc_silu(i)]}

            slots("bc", 0, {0: [dt_exp], 2: [dt_ln], 6: [acs_copy], 7: [ds_exp_]})
            with act.Fori(1, 4) as i:
                slots("bc", i, bc(i - 1))

            def xs_copy(g):
                need(act, mt_ready, 2 * g)
                need(act, states_done, g)
                if isinstance(g, int) and g == 0:
                    nat_copy("xz", 0, PACKS["bc"] + 8, rs_x, parity=0)
                else:
                    nat_copy("xz", g * 2, g * 6 + (PACKS["xz"] - 4), rs_x, parity=0)

            def xs_tap(g, j):
                need(act, yoff_done, g)
                conv_tap("xz", 6 * g + j, j, 2 * j, g * 4 + 2 * j)

            def xs_silu(g):
                act.wait_ge(xconv_done, 2 * g + 2)
                act.activation(conv, conv, ACT.Silu).then_inc(xs_act, 1)

            def xs_nat(g):
                need(act, xdt_ready, g)
                for t in range(NT):
                    act.wait_ge(tp_done, PACKS["xz"] + 6 * g + 3 + t)
                    copy(xs_n[:, t, :], ptr[:, t, :]).then_inc(tp_read, 1)

            def z_silu(g):
                group_ready("xz", 2 * g + 1)
                need(act, y_gated, g)
                for t in range(NT):
                    last = act.activation(s_z[:, t, :], acc_of(1, t), ACT.Silu, scale=rs_x[:, t:t + 1])
                last.then_inc(acc_read, 1)

            def bn_copy(g):
                act.wait_ge(cb_done, g + 1)
                need(act, states_done, g)
                copy(bn_sb, ptr[:, 0, 0:P]).then_inc(bn_ready, 1)

            def seg_exp(g, c):
                act.wait_ge(seg_done, 2 * g + c + 1)
                need(act, ydiag_done, 2 * g)
                act.activation(e_m[c].rearrange("p (h n) -> p h n", h=2), pss[:, :, :], ACT.Exp) \
                    .then_inc(exp_done, 1)

            def prev_copy(g):
                act.wait_ge(states_done, g + 1)
                copy(prev, ptr[:, 1, :]).then_inc(prev_ready, 1)

            def y_squares(g):
                act.wait_ge(y_gated, g + 1)
                for t in range(NT):
                    last = act.activation(junk[:, :], y_ssd[:, t, :], ACT.Square, accum_out=ss_g[:, t:t + 1])
                    act.drain() if t == 0 else None
                last.then_inc(gss_done, 1)

            def y_scale(g):
                act.wait_ge(gvar_done, g + 1)
                act.activation(rs_g, rs_g, ACT.Sqrt).then_inc(gsqrt_done, 1)
                act.wait_ge(grs_done, g + 1)
                for t in range(NT):
                    last = copy(y_ssd[:, t, :], y_ssd[:, t, :], rs_g[:, t:t + 1])
                last.then_inc(y_ready, 1)

            def ssd_hi(g):
                for j in range(2):
                    hi_pack("xz", 6 * g + 4 + j, j, 4 * g + (AT_SSD + 2 * j), 4 * g + (V_SSD + 2 * j))

            def during_z(g):
                return {1: [lambda: xs_copy(g)], 4: [lambda: xs_tap(g, 0), lambda: xs_tap(g, 1)],
                        7: [lambda: xs_silu(g)]}

            def during_xs(g):
                return {0: [lambda: xs_nat(g), lambda: z_silu(g)], 1: [lambda: seg_exp(g, 0)],
                        2: [lambda: bn_copy(g)], 3: [lambda: prev_copy(g)], 4: [lambda: seg_exp(g, 1)],
                        7: [lambda: y_squares(g)]}

            slots("xz", 0, bc(3))
            slots("xz", 1, during_z(0))
            with act.Fori(1, SG) as g:
                slots("xz", g * 2, during_xs(g - 1))
                slots("xz", g * 2 + 1, join({0: [lambda: y_scale(g - 1)], 2: [lambda: ssd_hi(g - 1)]}, during_z(g)))
            slots("sig_b", 0, during_xs(SG - 1))

            def sig_b_first():
                act.wait_ge(tp_done, PACKS["xz"] + 48)
                sig_to("sig_b", 0, sig_b)

            slots("sig_b", 1, {0: [lambda: y_scale(SG - 1)], 2: [lambda: ssd_hi(SG - 1)], 4: [sig_b_first]})
            with act.Fori(2, 4) as i:
                slots("sig_b", i, {1: [lambda: sig_to("sig_b", i - 1, sig_b)]})

            def merge_hi(i):
                for j in range(2):
                    hi_pack("ssd_out", 2 * i + j, j, 4 * i + (AT_X + 2 * j))

            slots("ssd_out", 0, {1: [lambda: sig_to("sig_b", 3, sig_b)]})
            with act.Fori(1, 4) as i:
                slots("ssd_out", i, {3: [lambda: merge_hi(i - 1)]})

            def mem_squares():
                act.drain()
                act.wait_ge(in_mem, 16)
                for t in range(NT):
                    for j in range(4):
                        act.activation(junk[:, :], mem_n[:, t, j * N:(j + 1) * N], ACT.Square,
                                       accum_out=ss_ff4[:, t * 4 + j:t * 4 + j + 1])
                        act.drain()
                act.nop().then_inc(ss_done, 1)

            def mem_hi(lo, hi):
                for m in range(lo, hi):
                    hi_pack("mem", m, m % 2, AT_MEM + 2 * m, V_MEM + 2 * m)

            def h_save(base, i, ss4):
                act.wait_ge(hg_ready, base + i + 1)
                o = hres[:, :, i * N:(i + 1) * N] if isinstance(i, int) else hres[:, :, ds(i * N, N)]
                copy(o, nat[:, :, :])
                for t in range(NT):
                    a = ss4[:, 2 * i + t:2 * i + t + 1] if isinstance(i, int) else ss4[:, ds(i * 2 + t, 1)]
                    last = act.activation(junk[:, :], nat[:, t, :], ACT.Square, accum_out=a)
                    act.drain() if t == 0 else None
                last.then_inc(h_saved, 1)

            def h_hi(phase, i, at, col):
                for j in range(2):
                    hi_pack(phase, 2 * i + j, j, 4 * i + (at + 2 * j), 4 * i + (col + 2 * j))

            def mix(i):
                return {0: [lambda: h_save(0, i, ss_xa4)], 2: [lambda: h_hi("mix", i, AT_XA, V_XA)]}

            slots("mix", 0, {2: [lambda: merge_hi(3)], 5: [lambda: mem_hi(0, 2)], 6: [lambda: mem_hi(2, 4)],
                             7: [lambda: mem_hi(4, 6)]})
            slots("mix", 1, join({0: [lambda: mem_hi(6, 8)]}, mix(0), {4: [mem_squares], 6: [lambda: root(3, rs_mem)]}))
            with act.Fori(2, 4) as i:
                slots("mix", i, mix(i - 1))

            def v_copy(i):
                group_ready("xv", i)
                for t in range(NT):
                    o = v_x[:, t, i * N:(i + 1) * N] if isinstance(i, int) else v_x[:, t, ds(i * N, N)]
                    last = copy(o, acc_of(i, t), rs_mem[:, t:t + 1])
                last.then_inc(acc_read, 1)

            def v_first():
                act.wait_ge(merged_ready, 4)
                act.wait_ge(rs_done, 3)
                v_copy(0)

            slots("xv", 0, {**mix(3), 5: [lambda: root(4, rs_xa)]})
            slots("xv", 1, {1: [v_first]})
            with act.Fori(2, 4) as i:
                slots("xv", i, {1: [lambda: v_copy(i - 1)]})

            def k_copy(n):
                m = PACKS["mix"] + 8 if isinstance(n, int) and n == 0 else n * 6 + (PACKS["kq"] - 2)
                nat_copy("kq", 2 * n, m, rs_mem, parity=0)

            def turned(m, n, dst, prior=None):
                for j in range(2):
                    act.wait_ge(tp_done, PACKS["kq"] + 6 * n + m + j + 1)
                    copy(dst[:, 2 * j:2 * j + 2, :], ptr[:, j, :].rearrange("p (k n) -> p k n", k=2)) \
                        .then_inc(tp_read, 1)

            def k_turned(n):
                need(act, xscores_done, n)
                turned(0, n, kx_t)

            def q_copy(n):
                nat_copy("kq", 2 * n + 1, PACKS["kq"] + 6 * n + 2, rs_xa, parity=1)

            def q_turned(n):
                turned(2, n, qx_t)

            def softmax_exp(n):
                act.wait_ge(nmx_ready, n + 1)
                need(act, pt_done, n)
                for t in range(NT):
                    last = act.activation(prob[:, t, :], pss[:, 0, t * T:(t + 1) * T], ACT.Exp,
                                          bias=nmx[:, t:t + 1], scale=XD ** -0.5, accum_out=sm[:, t:t + 1])
                last.then_inc(prob_ready, 1)

            def p_copy(n):
                act.wait_ge(pt_done, n + 1)
                copy(prob_t, pss[:, 1, :]).then_inc(pt_copied, 1)

            def o_hi(n):
                for j in range(2):
                    hi_pack("kq", 6 * n + 4 + j, j, 4 * n + (AT_X + 2 * j))

            def attention(n):
                return {0: [lambda: q_copy(n)], 1: [lambda: q_turned(n)], 2: [lambda: softmax_exp(n)],
                        3: [lambda: p_copy(n)], 5: [lambda: o_hi(n)]}

            slots("kq", 0, {1: [lambda: v_copy(3)]})
            slots("kq", 1, {1: [lambda: k_copy(0)], 2: [lambda: k_turned(0)]})
            with act.Fori(1, XH) as n:
                slots("kq", n * 2, attention(n - 1))
                slots("kq", n * 2 + 1, {1: [lambda: k_copy(n)], 2: [lambda: k_turned(n)]})

            def xo(i):
                return {0: [lambda: h_save(4, i, ss_ff4)], 2: [lambda: h_hi("xo", i, AT_FF, V_FF)]}

            slots("xo", 0, attention(XH - 1))
            with act.Fori(1, 4) as i:
                slots("xo", i, xo(i - 1))

            def relu(phase, i):
                group_ready(phase, i)
                need(act, sq_ready, (8 if phase == "ff1b" else 0) + i)
                for t in range(NT):
                    last = act.activation(nat[:, t, :], acc_of(i, t), ACT.Relu, scale=rs_ff[:, t:t + 1])
                last.then_inc(acc_read, 1)

            def sq_hi(phase, i):
                for j in range(2):
                    hi_pack(phase, 2 * i + j, j, 4 * i + (AT_HID + 2 * j))

            def relu_first():
                act.wait_ge(rs_done, 5)
                relu("ff1a", 0)

            def up(phase, i):
                return {0: [lambda: relu(phase, i)], 2: [lambda: sq_hi(phase, i)]}

            slots("ff1a", 0, {**xo(3), 5: [lambda: root(5, rs_ff)]})
            slots("ff1a", 1, {0: [relu_first], 2: [lambda: sq_hi("ff1a", 0)]})
            with act.Fori(2, 8) as i:
                slots("ff1a", i, up("ff1a", i - 1))
            slots("ff2a", 0, up("ff1a", 7))
            with act.Fori(1, 4) as i:
                slots("ff2a", i, {})
            slots("ff1b", 0, {})
            with act.Fori(1, 8) as i:
                slots("ff1b", i, up("ff1b", i - 1))
            slots("ff2b", 0, up("ff1b", 7))
            with act.Fori(1, 3) as i:
                slots("ff2b", i, {})
            slots("ff2b", 3, {}, final=True)

            act.wait_ge(acc_read, GROUP["ff2b"] + 4)
            act.wait_ge(in_fn, 16)
            for t in range(NT):
                last = act.activation(reg_c[:, D:2 * D], hres[:, t, :], ACT.Square, accum_out=ss_out[:, t:t + 1])
                act.drain() if t == 0 else None
            last.then_inc(ss_done, 1)
            root(6, rs_out)

        @block.vector
        def _(dve):
            def tt(o, a, b, op):
                return dve.tensor_tensor(o, a, b, op)

            def split_lo(phase, i, c):
                n = CHUNK[phase] + CPG[phase] * i + c + LEAD
                s = (c + LEAD) % RAW
                dve.wait_ge(hi_ready, n + 1)
                tt(w_lo[:, s, :], raw[:, s, :], w_hi[:, s, :].bitcast(F32), ALU.subtract).then_inc(lo_ready, 1)

            def slots(phase, i, hooks, final=False):
                for c in range(CPG[phase]):
                    if not (final and c + LEAD >= CPG[phase]):
                        split_lo(phase, i, c)
                    if c in hooks:
                        dve.drain()
                    for step in hooks.get(c, ()):
                        step()

            def group_ready(phase, i):
                dve.wait_ge(w_used, group_end(phase, i))
                need(dve, acc_read, GROUP[phase] + i)

            def lo_pack(split, m, b, at, col=None):
                dve.wait_ge(tp_hi, SPLITS[split] + m + 1)
                if col is None:
                    a = slice(at, at + 2) if isinstance(at, int) else ds(at, 2)
                    tt(acts_lo[:, a, :], ptr[:, b, :].rearrange("p (k n) -> p k n", k=2),
                       acts_hi[:, a, :].bitcast(F32), ALU.subtract).then_inc(tp_read, 1)
                    return
                for k in range(2):
                    a, v = at + k, col + k
                    if isinstance(a, int):
                        lo, hi = acts_lo[:, a, :], acts_hi[:, a, :]
                    else:
                        lo = acts_lo[:, ds(a, 1), :].rearrange("p a n -> p (a n)")
                        hi = acts_hi[:, ds(a, 1), :].rearrange("p a n -> p (a n)")
                    sc = vec[:, v:v + 1] if isinstance(v, int) else vec[:, ds(v, 1)]
                    last = dve.scalar_tensor_tensor(lo, ptr[:, b, k * T:(k + 1) * T], sc, hi.bitcast(F32),
                                                    ALU.mult, ALU.subtract)
                last.then_inc(tp_read, 1)

            def mean_square(ss, out_, width):
                return dve.tensor_scalar(out_, ss, 1.0 / width, EPS, ALU.mult, ALU.add)

            def rstd(n, v):
                dve.wait_ge(sqrt_done, n)
                dve.reciprocal(v, v).then_inc(rs_done, 1)
                dve.drain()

            dve.wait_ge(vec_turned, 1)
            dve.tensor_copy(vec[:, :], pss[:, 0, 0:V_ALL]).then_inc(vec_ready, 1)
            for n in range(LEAD):
                dve.wait_ge(hi_ready, n + 1)
                tt(w_lo[:, n, :], raw[:, n, :], w_hi[:, n, :].bitcast(F32), ALU.subtract).then_inc(lo_ready, 1)
            dve.drain()
            for m in range(8):
                lo_pack("x", m, m % 2, AT_X + 2 * m, V_MIX + 2 * m)
            dve.wait_ge(ss_done, 1)
            mean_square(ss_x, rs_x, D).then_inc(var_done, 1)

            def rotate(i):
                dve.wait_ge(acc_read, GROUP["qkv"] + i + 1)
                need(dve, qk_turned, i)
                need(dve, scores_done, i)
                qk = qkv[:, :, 0:2 * DK].rearrange("p t (a d) -> p t a d", a=4)
                tt(rot_a, qk, cos.broadcast_to([P, NT, 4, DK // 2]), ALU.mult)
                tt(rot_b, qk, sin.broadcast_to([P, NT, 4, DK // 2]), ALU.mult)
                dve.drain()
                a2 = rot_a.rearrange("p t (a h) d -> p (t a) h d", h=2)
                b2 = rot_b.rearrange("p t (a h) d -> p (t a) h d", h=2)
                r2 = rot.rearrange("p t (a h) d -> p (t a) h d", h=2)
                tt(r2[:, :, 0, :], a2[:, :, 0, :], b2[:, :, 1, :], ALU.subtract)
                tt(r2[:, :, 1, :], a2[:, :, 1, :], b2[:, :, 0, :], ALU.add).then_inc(rotated, 1)
                dve.drain()
                z = cst[:, C_ZETA + i:C_ZETA + i + 1] if isinstance(i, int) else cst[:, ds(i + C_ZETA, 1)]
                dve.tensor_scalar(k_z, rotm[:, 0, 1, :], z, None, ALU.mult).then_inc(kz_ready, 1)

            def decay_scores(i):
                dve.wait_ge(scores_done, i + 1)
                need(dve, inner_done, i)
                d = dec_t[:, i:i + 1, :] if isinstance(i, int) else dec_t[:, ds(i, 1), :]
                tt(s_t, pss[:, 1, 0:T].rearrange("p (c n) -> p c n", c=NT), d.broadcast_to([P, NT, P]), ALU.mult) \
                    .then_inc(decayed, 1)

            def ret_y(i):
                dve.wait_ge(inner_done, i + 1)
                cols = slice(i * DV, (i + 1) * DV) if isinstance(i, int) else ds(i * DV, DV)
                dve.tensor_copy(y_ret[:, 0, cols], ptr[:, 0, 0:DV])
                dve.wait_ge(cross_copied, i + 1)
                tt(y_ret[:, 1, cols], ptr[:, 0, DV:2 * DV], cross_sb, ALU.add)
                dve.drain()
                for t in range(NT):
                    dve.bn_stats(bnst[:, t, :], y_ret[:, t, cols])
                dve.drain()
                for t in range(NT):
                    dve.bn_aggr(bnag[:, 2 * t:2 * t + 2], bnst[:, t, :])
                dve.drain()
                m = mv[:, 4 * i:4 * i + 4] if isinstance(i, int) else mv[:, ds(i * 4, 4)]
                dve.tensor_copy(m, bnag).then_inc(y_stored, 1)
                dve.drain()

            def retention(i):
                return {0: [lambda: rotate(i)], 4: [lambda: decay_scores(i)], 6: [lambda: ret_y(i)]}

            slots("qkv", 0, {1: [lambda: rstd(1, rs_x), lambda: dve.wait_ge(in_dec, 16)]})
            with dve.Fori(1, HEADS) as i:
                slots("qkv", i, retention(i - 1))

            def head_vars():
                v = mv.rearrange("p (j s) -> p j s", s=2)[:, :, 1]
                dve.tensor_scalar(rgn, v, EPS, None, ALU.add).then_inc(var_done, 1)

            def gate_mul(i):
                for t in range(NT):
                    for h in range(2):
                        if isinstance(i, int):
                            y = y_ret[:, t, i * N + h * DV:i * N + (h + 1) * DV]
                            j = 4 * i + 2 * h + t
                            mu, r = mv[:, 2 * j:2 * j + 1], rgn[:, j:j + 1]
                        else:
                            y = y_ret[:, t, ds(i * N + h * DV, DV)]
                            mu, r = mv[:, ds(i * 8 + (4 * h + 2 * t), 1)], rgn[:, ds(i * 4 + (2 * h + t), 1)]
                        dve.tensor_scalar(y, y, mu, r, ALU.subtract, ALU.mult)
                dve.drain()
                dve.wait_ge(acc_read, GROUP["gate"] + i + 1)
                cols = slice(i * N, (i + 1) * N) if isinstance(i, int) else ds(i * N, N)
                tt(gated, y_ret[:, :, cols], gated, ALU.mult).then_inc(gated_ready, 1)

            def gate_lo(i):
                for j in range(2):
                    lo_pack("gate", 2 * i + j, j, 4 * i + (AT_RET + 2 * j), 4 * i + (V_RET + 2 * j))

            def gate(i):
                return {0: [lambda: gate_mul(i)], 3: [lambda: gate_lo(i)]}

            slots("gate", 0, join(retention(HEADS - 1), {6: [head_vars], 7: [lambda: rstd(2, rgn)]}))
            with dve.Fori(1, 4) as i:
                slots("gate", i, gate(i - 1))
            slots("sig_a", 0, gate(3))
            with dve.Fori(1, 4) as i:
                slots("sig_a", i, {})

            def branch_a(i):
                group_ready("ret_out", i)
                cols = slice(i * N, (i + 1) * N) if isinstance(i, int) else ds(i * N, N)
                tt(merged[:, :, cols], acc_both(i), sig_a[:, :, cols], ALU.mult).then_inc(acc_read, 1)

            slots("ret_out", 0, {})
            with dve.Fori(1, 4) as i:
                slots("ret_out", i, {1: [lambda: branch_a(i - 1)]})
            slots("dt", 0, {1: [lambda: branch_a(3)]})

            wk = junk[:, :].rearrange("p (a t n) -> p a t n", a=4, t=NT)

            def dt_in():
                dve.wait_ge(w_used, CHUNK["dt"] + CPG["dt"])
                dve.wait_ge(in_head, 48)
                for t in range(NT):
                    dve.scalar_tensor_tensor(wk[:, 0, t], pss[:, t, 0:SH], rs_x[:, t:t + 1], headrow[:, 0, :],
                                             ALU.mult, ALU.add)
                dve.drain()
                dve.scalar_tensor_tensor(wk[:, 1], wk[:, 0], -1.0, wk[:, 0], ALU.mult, ALU.min).then_inc(dt_1, 1)

            def dt_w():
                dve.wait_ge(dt_2, 2)
                dve.tensor_scalar(wk[:, 2], wk[:, 1], 1.0, None, ALU.add).then_inc(dt_3, 1)

            def dt_out():
                dve.wait_ge(dt_4, 1)
                dve.tensor_scalar(wk[:, 2], wk[:, 2], 1.0, None, ALU.subtract)
                dve.drain()
                dve.tensor_scalar(da[:, :, :], wk[:, 2], 0.0, None, ALU.is_equal)
                dve.drain()
                tt(wk[:, 2], wk[:, 2], da[:, :, :], ALU.add)
                tt(da[:, :, :], da[:, :, :], wk[:, 1], ALU.mult)
                dve.drain()
                dve.reciprocal(wk[:, 2], wk[:, 2])
                tt(wk[:, 3], wk[:, 3], wk[:, 1], ALU.mult)
                dve.drain()
                tt(wk[:, 3], wk[:, 3], wk[:, 2], ALU.mult)
                dve.drain()
                tt(wk[:, 3], wk[:, 3], da[:, :, :], ALU.add)
                dve.drain()
                dve.scalar_tensor_tensor(dtt[:, :, :], wk[:, 0], 0.0, wk[:, 3], ALU.max, ALU.add)
                dve.drain()
                for t in range(NT):
                    last = dve.scalar_tensor_tensor(da[:, t, :], dtt[:, t, :], -1.0, headrow[:, 1, :],
                                                    ALU.mult, ALU.mult)
                last.then_inc(da_ready, 1)

            def to_end():
                dve.wait_ge(acs_copied, 1)
                tt(dstate[:, :], junk[:, 2 * SH:3 * SH], junk[:, 0:SH], ALU.subtract).then_inc(ds_ready, 1)

            def conv_pack(b, q0, ct):
                def col(v, k):
                    v = ct + (v + k)
                    return vec[:, v:v + 1] if isinstance(v, int) else vec[:, ds(v, 1)]
                for j in range(2, -1, -1):
                    back = 3 - j
                    for k in range(2):
                        src, o = ptr[:, b, k * T:(k + 1) * T], conv[:, q0 + k, :]
                        last = dve.scalar_tensor_tensor(o[:, back:], src[:, 0:T - back],
                                                        col(V_CW + j * (CONV // P), k), o[:, back:],
                                                        ALU.mult, ALU.add)
                    if j:
                        dve.drain()
                return last

            def bc_conv(i):
                for j in range(2):
                    dve.wait_ge(tap_done, 2 * i + j + 1)
                    conv_pack(j, 2 * j, i * 4 + (INNER // P + 2 * j)).then_inc(tp_read, 1)
                dve.drain()
                dve.nop().then_inc(conv_done, 1)

            slots("bc", 0, {0: [dt_in], 1: [dt_w], 4: [dt_out], 6: [to_end]})
            with dve.Fori(1, 4) as i:
                slots("bc", i, {4: [lambda: bc_conv(i - 1)]})

            def by_head(ap, g, cnt):
                a = ap[:, g * RH:(g + 1) * RH] if isinstance(g, int) else ap[:, ds(g * RH, RH)]
                return a.rearrange("p (r a) -> p r a", a=1).broadcast_to([P, RH, cnt])

            def xs_conv(g, j):
                dve.wait_ge(tap_done, 8 + 2 * g + j + 1)
                conv_pack(j, 2 * j, g * 4 + 2 * j).then_inc(tp_read, 1)
                dve.drain()
                dve.nop().then_inc(xconv_done, 1)

            def heads3(ap):
                return ap.rearrange("p (r d) -> p r d", r=RH)

            def xdt_mul(g):
                dve.wait_ge(tp_read, PACKS["xz"] + 6 * g + 4)
                need(dve, ydiag_done, 2 * g)
                for t in range(NT):
                    tt(heads3(xdt[:, t, :]), heads3(xs_n[:, t, :]), by_head(dtt[:, t, :], g, SP_), ALU.mult)
                need(dve, tp_done, PACKS["xz"] + 6 * g)
                for t in range(NT):
                    tt(heads3(y_ssd[:, t, :]), heads3(xs_n[:, t, :]), by_head(headrow[:, 2, :], g, SP_), ALU.mult)
                dve.drain()
                tt(heads3(xdtd), heads3(xdt[:, 0, :]), by_head(dstate[:, :], g, SP_), ALU.mult) \
                    .then_inc(xdt_ready, 1)

            def tri_da(g, c):
                need(dve, seg_done, 2 * g + c)
                tt(d_tri.rearrange("p (r l) -> p r l", r=RH),
                   tri.rearrange("p (a l) -> p a l", a=1).broadcast_to([P, RH, P]),
                   by_head(da[:, c, :], g, P), ALU.mult).then_inc(dtri_ready, 1)

            def mask_cb(g):
                dve.wait_ge(cb_done, g + 1)
                dve.wait_ge(bn_ready, g + 1)
                tt(cbm, ptr[:, 0, P:3 * P].rearrange("p (c l) -> p c l", c=NT),
                   tri.rearrange("p (a l) -> p a l", a=1).broadcast_to([P, NT, P]), ALU.mult) \
                    .then_inc(cbm_ready, 1)

            def decay_cb(g, c):
                dve.wait_ge(exp_done, 2 * g + c + 1)
                e3 = e_m[c].rearrange("p (r l) -> p r l", r=RH)
                tt(e3, e3, cbm[:, c:c + 1, :].broadcast_to([P, RH, P]), ALU.mult).then_inc(mt_ready, 1)

            def add_y0(g):
                dve.wait_ge(ydiag_done, 2 * g + 1)
                tt(y_ssd[:, 0, :], ptr[:, 0, :], y_ssd[:, 0, :], ALU.add).then_inc(y_added, 1)

            def add_off(g):
                dve.wait_ge(yoff_done, g + 1)
                tt(heads3(junk[:, :]), heads3(ptr[:, 1, :]), by_head(eacs[:, :], g, SP_), ALU.mult)
                dve.drain()
                tt(y_ssd[:, 1, :], junk[:, :], y_ssd[:, 1, :], ALU.add).then_inc(y_added, 1)

            def add_y1(g):
                dve.drain()
                dve.wait_ge(ydiag_done, 2 * g + 2)
                tt(y_ssd[:, 1, :], ptr[:, 0, :], y_ssd[:, 1, :], ALU.add).then_inc(y_added, 1)
                dve.drain()
                dve.wait_ge(acc_read, GROUP["xz"] + 2 * g + 2)
                tt(y_ssd, y_ssd, s_z, ALU.mult).then_inc(y_gated, 1)

            def y_rstd(g):
                dve.wait_ge(gss_done, g + 1)
                mean_square(ss_g, rs_g, N).then_inc(gvar_done, 1)
                dve.wait_ge(gsqrt_done, g + 1)
                dve.reciprocal(rs_g, rs_g).then_inc(grs_done, 1)

            def ssd_lo(g):
                for j in range(2):
                    lo_pack("xz", 2 * g + j, j, 4 * g + (AT_SSD + 2 * j), 4 * g + (V_SSD + 2 * j))

            def during_z(g):
                return {4: [lambda: xs_conv(g, 0)], 5: [lambda: xs_conv(g, 1)], 7: [lambda: tri_da(g, 0)]}

            def during_xs(g):
                return {0: [lambda: xdt_mul(g)], 1: [lambda: tri_da(g, 1)], 2: [lambda: mask_cb(g)],
                        3: [lambda: decay_cb(g, 0)], 5: [lambda: add_y0(g), lambda: decay_cb(g, 1)],
                        6: [lambda: add_off(g)], 7: [lambda: add_y1(g)]}

            def before_ssd():
                dve.wait_ge(ds_exp, 1)
                dve.wait_ge(m_stored, 16)

            slots("xz", 0, {4: [lambda: bc_conv(3), before_ssd]})
            slots("xz", 1, during_z(0))
            with dve.Fori(1, SG) as g:
                slots("xz", g * 2, during_xs(g - 1))
                slots("xz", g * 2 + 1, join({0: [lambda: y_rstd(g - 1)], 2: [lambda: ssd_lo(g - 1)]}, during_z(g)))
            slots("sig_b", 0, during_xs(SG - 1))
            slots("sig_b", 1, {0: [lambda: y_rstd(SG - 1)], 2: [lambda: ssd_lo(SG - 1)]})
            with dve.Fori(2, 4) as i:
                slots("sig_b", i, {})

            def merge(i):
                group_ready("ssd_out", i)
                cols = slice(i * N, (i + 1) * N) if isinstance(i, int) else ds(i * N, N)
                tt(sig_b[:, :, cols], acc_both(i), sig_b[:, :, cols], ALU.mult).then_inc(acc_read, 1)
                dve.drain()
                need(dve, tp_done, PACKS["ssd_out"] + 2 * i)
                tt(nat[:, :, :], sig_b[:, :, cols], merged[:, :, cols], ALU.add).then_inc(merged_ready, 1)

            def merge_lo(i):
                for j in range(2):
                    lo_pack("ssd_out", 2 * i + j, j, 4 * i + (AT_X + 2 * j))

            slots("ssd_out", 0, {5: [lambda: dve.wait_ge(in_m, 16)]})
            with dve.Fori(1, 4) as i:
                slots("ssd_out", i, {1: [lambda: merge(i - 1)], 3: [lambda: merge_lo(i - 1)]})

            def mem_lo(lo, hi):
                for m in range(lo, hi):
                    lo_pack("mem", m, m % 2, AT_MEM + 2 * m, V_MEM + 2 * m)

            def sum4(ss4, pattern, out_, width):
                dve.tensor_reduce(out_, ss4.rearrange(pattern, t=NT), axis=AX.X, op=ALU.add)
                dve.drain()
                mean_square(out_, out_, width).then_inc(var_done, 1)

            def mem_var():
                dve.wait_ge(ss_done, 2)
                sum4(ss_ff4, "p (t j) -> p t j", rs_mem, D)

            def h_add(phase, base, i, m):
                group_ready(phase, i)
                need(dve, tp_done, m)
                need(dve, h_saved, base + i)
                cols = slice(i * N, (i + 1) * N) if isinstance(i, int) else ds(i * N, N)
                tt(nat[:, :, :], acc_both(i), hres[:, :, cols], ALU.add).then_inc(acc_read, 1)

            def h_lo(phase, i, at, col):
                for j in range(2):
                    lo_pack(phase, 2 * i + j, j, 4 * i + (at + 2 * j), 4 * i + (col + 2 * j))

            def mix_add(i):
                first = isinstance(i, int) and i == 0
                h_add("mix", 0, i, PACKS["ssd_out"] + 8 if first else PACKS["mix"] + 2 * i)
                dve.drain()
                dve.nop().then_inc(hg_ready, 1)

            slots("mix", 0, {1: [lambda: merge(3)], 2: [lambda: merge_lo(3)], 5: [lambda: mem_lo(0, 2)],
                             6: [lambda: mem_lo(2, 4)], 7: [lambda: mem_lo(4, 6)]})

            def mix(i):
                return {0: [lambda: mix_add(i)], 2: [lambda: h_lo("mix", i, AT_XA, V_XA)]}

            slots("mix", 1, join({0: [lambda: mem_lo(6, 8), lambda: dve.wait_ge(in_h, 16)]}, mix(0),
                                 {5: [mem_var], 7: [lambda: rstd(3, rs_mem)]}))
            with dve.Fori(2, 4) as i:
                slots("mix", i, mix(i - 1))

            def xa_var():
                dve.wait_ge(h_saved, 4)
                sum4(ss_xa4, "p (j t) -> p t j", rs_xa, D)

            slots("xv", 0, {**mix(3), 4: [xa_var], 6: [lambda: rstd(4, rs_xa)]})
            with dve.Fori(1, 4) as i:
                slots("xv", i, {})

            def softmax_max(n):
                dve.wait_ge(xscores_done, n + 1)
                dve.reduce_max(mx, pss[:, 0, :].rearrange("p (t m) -> p t m", t=NT), AX.X)
                dve.drain()
                dve.tensor_scalar(nmx, mx, -(XD ** -0.5), None, ALU.mult).then_inc(nmx_ready, 1)

            def o_scale(n):
                dve.wait_ge(prob_ready, n + 1)
                dve.reciprocal(rsm, sm)
                dve.drain()
                dve.wait_ge(pv_done, n + 1)
                need(dve, tp_done, PACKS["kq"] + 6 * n)
                for t in range(NT):
                    last = dve.tensor_scalar(o_n[:, t, :], pss[:, t, :], rsm[:, t:t + 1], None, ALU.mult)
                last.then_inc(o_ready, 1)

            def o_lo(n):
                for j in range(2):
                    lo_pack("kq", 2 * n + j, j, 4 * n + (AT_X + 2 * j))

            def attention(n):
                return {1: [lambda: softmax_max(n)], 3: [lambda: o_scale(n)], 5: [lambda: o_lo(n)]}

            slots("kq", 0, {})
            slots("kq", 1, {})
            with dve.Fori(1, XH) as n:
                slots("kq", n * 2, attention(n - 1))
                slots("kq", n * 2 + 1, {})
            slots("xo", 0, attention(XH - 1))

            def xo_add(i):
                first = isinstance(i, int) and i == 0
                h_add("xo", 4, i, PACKS["kq"] + 24 if first else PACKS["xo"] + 2 * i)
                dve.drain()
                dve.nop().then_inc(hg_ready, 1)

            def xo(i):
                return {0: [lambda: xo_add(i)], 2: [lambda: h_lo("xo", i, AT_FF, V_FF)]}

            with dve.Fori(1, 4) as i:
                slots("xo", i, xo(i - 1))

            def ff_var():
                dve.wait_ge(h_saved, 8)
                sum4(ss_ff4, "p (j t) -> p t j", rs_ff, D)

            def square(phase, i):
                dve.wait_ge(acc_read, GROUP[phase] + i + 1)
                need(dve, tp_done, (PACKS["xo"] + 8 if isinstance(i, int) and i == 0 and phase == "ff1a"
                                    else PACKS[phase] + 2 * i))
                tt(sq_n, nat[:, :, :], nat[:, :, :], ALU.mult).then_inc(sq_ready, 1)

            def sq_lo(phase, i):
                for j in range(2):
                    lo_pack(phase, 2 * i + j, j, 4 * i + (AT_HID + 2 * j))

            def up(phase, i):
                return {0: [lambda: square(phase, i)], 2: [lambda: sq_lo(phase, i)]}

            def down_add(phase, i):
                group_ready(phase, i)
                cols = slice(i * N, (i + 1) * N) if isinstance(i, int) else ds(i * N, N)
                tt(hres[:, :, cols], acc_both(i), hres[:, :, cols], ALU.add).then_inc(acc_read, 1)

            slots("ff1a", 0, {**xo(3), 4: [ff_var], 6: [lambda: rstd(5, rs_ff)]})
            with dve.Fori(1, 8) as i:
                slots("ff1a", i, up("ff1a", i - 1))
            slots("ff2a", 0, up("ff1a", 7))
            with dve.Fori(1, 4) as i:
                slots("ff2a", i, {1: [lambda: down_add("ff2a", i - 1)]})
            slots("ff1b", 0, {1: [lambda: down_add("ff2a", 3)]})
            with dve.Fori(1, 8) as i:
                slots("ff1b", i, up("ff1b", i - 1))
            slots("ff2b", 0, up("ff1b", 7))
            with dve.Fori(1, 3) as i:
                slots("ff2b", i, {1: [lambda: down_add("ff2b", i - 1)]})
            slots("ff2b", 3, {1: [lambda: down_add("ff2b", 2)]}, final=True)
            down_add("ff2b", 3)

            dve.wait_ge(ss_done, 3)
            mean_square(ss_out, rs_out, D).then_inc(var_done, 1)
            rstd(6, rs_out)
            dve.wait_ge(in_fn, 16)
            for t in range(NT):
                dve.scalar_tensor_tensor(hres[:, t, :], hres[:, t, :], rs_out[:, t:t + 1], fnw,
                                         ALU.mult, ALU.mult).then_inc(h_done, 1)


def constants():
    f = np.float32
    c = np.zeros((P, C_ALL), f)
    i = np.arange(P)
    c[:, C_ID:C_ID + P] = np.eye(P, dtype=f)
    c[:, C_TRI:C_TRI + P] = i[:, None] <= i[None, :]
    c[:, C_TGT:C_TGT + P] = i[:, None] > i[None, :]
    c[:, C_ONE:C_ONE + P] = 1.0
    half = DK // 2
    inv = np.exp(f(-math.log(10000.0)) * np.arange(half, dtype=f) / f(half)).astype(f)
    ang = (np.arange(T, dtype=f)[:, None] * inv[None, :]).astype(f)
    for at, fn in ((C_COS, np.cos), (C_SIN, np.sin)):
        c[:, at:at + P] = fn(ang.astype(np.float64)).astype(f).reshape(NT, P, half).transpose(1, 0, 2).reshape(P, P)
    log_g = np.log(f(1.0) - np.exp2(f(-5.0) - np.arange(HEADS, dtype=f))).astype(f)
    idx = np.arange(P, dtype=f)
    c[:, C_ZETA:C_ZETA + HEADS] = np.exp((f(P - 1) - idx)[:, None] * log_g[None, :])
    c[:, C_XI:C_XI + HEADS] = np.exp((idx + f(1))[:, None] * log_g[None, :]) 
    rel = idx[None, :] - idx[:, None]
    dec = np.where(rel[:, None, :] >= 0, np.exp(np.maximum(rel, 0)[:, None, :] * log_g[None, :, None]), 0)
    return c, dec.astype(f).reshape(P, HEADS * P)


_INS = ['x', 'mem', 'w_in', 'conv_w', 'conv_b', 'dt_bias', 'a_log', 'd_skip', 'norm_mix_w', 'ret_norm_w',
        'ssd_norm_w', 'w_ret_out', 'w_ssd_out', 'w_mix_out', 'norm_xa_w', 'mem_norm_w', 'w_xq', 'w_xkv', 'w_xo',
        'norm_ff_w', 'w_ff1', 'w_ff2', 'final_norm_w']


def kernel(**inputs):
    import concourse.bacc as _bacc
    from concourse.bass_utils import run_bass_kernel_spmd as _run

    nc = _bacc.Bacc("TRN2", target_bir_lowering=False, num_devices=1)
    arrays, args = {}, {}

    def give(name, a):
        arrays[f"in_{name}"] = a
        args[name] = nc.dram_tensor(f"in_{name}", a.shape, mybir.dt.from_np(a.dtype), kind="ExternalInput").ap()

    for name in _INS:
        give(name, np.ascontiguousarray(inputs[name]))
    cst, dec = constants()
    give("consts", cst)
    give("decay", dec)
    args["merged_dram"] = nc.dram_tensor("merged_dram", (P, NT * D), F32, kind="Internal").ap()
    args["out"] = nc.dram_tensor("out_0", (1, T, D), F32, kind="ExternalOutput").ap()
    hybrid_layer(nc, **args)
    r = _run(nc, [arrays], core_ids=[0])
    return r.results[0]["out_0"]
```

```python
import math
from contextlib import ExitStack

import numpy as np

import concourse.bass as bass
from concourse import mybir

F32 = mybir.dt.float32
F32R = mybir.dt.float32r
ALU = mybir.AluOpType
ACT = mybir.ActivationFunctionType
AX = mybir.AxisListType
ds = bass.ds

P = 128
D = 2048
T = 256
NT = T // P
KT = D // P
EPS = 1e-6
HEADS, DK, DV = 8, 128, 256
INNER, SH, SP_, SG, SN = 4096, 64, 64, 8, 128
RH = SH // SG
CONV = INNER + 2 * SG * SN
XH, XD = 4, 512
FF = 8192
N = 512
CK = 2
RAW, RING, LEAD = 4, 4, 3

V0 = 2 * HEADS * DK
G0 = V0 + HEADS * DV
Z0 = G0 + HEADS * DV
X0 = Z0 + INNER
B0 = X0 + INNER
DT0 = X0 + CONV
GA0 = DT0 + SH
GB0 = GA0 + D

V_MIX, V_XA, V_MEM, V_FF, V_RET, V_SSD, V_CB, V_CW = 0, 16, 32, 48, 64, 80, 112, 160
V_ALL = V_CW + 4 * (CONV // P)

C_ID, C_TRI, C_ONE, C_COS, C_SIN, C_ZETA, C_XI = 0, 128, 256, 384, 512, 640, 648
C_ALL = 656

PHASES = [("qkv", 8, 8), ("gate", 4, 8), ("sig_a", 4, 8), ("ret_out", 4, 8), ("dt", 0, 4), ("bc", 4, 8),
          ("xz", 16, 8), ("sig_b", 4, 8), ("ssd_out", 4, 16), ("mix", 4, 8), ("xv", 4, 8), ("kq", 8, 8),
          ("xo", 4, 8), ("ff1a", 8, 8), ("ff2a", 4, 16), ("ff1b", 8, 8), ("ff2b", 4, 16)]
CHUNK, GROUP = {}, {}
_c = _g = 0
for _n, _k, _s in PHASES:
    CHUNK[_n], GROUP[_n] = _c, _g
    _c += max(_k, 1) * _s
    _g += _k
CPG = {n: s for n, _, s in PHASES}
COUNT = {n: k for n, k, _ in PHASES}
PACKS, SPLITS = {}, {}
_c = _g = 0
for _n, _k, _s in [("x", 8, 8), ("gate", 8, 8), ("bc", 8, 0), ("xz", 48, 16), ("ssd_out", 8, 8), ("mem", 8, 8),
                   ("mix", 8, 8), ("kq", 24, 8), ("xo", 8, 8), ("ff1a", 16, 16), ("ff1b", 16, 16)]:
    PACKS[_n], SPLITS[_n] = _c, _g
    _c += _k
    _g += _s
AT_RET, AT_SSD, AT_MEM, AT_XA, AT_FF, AT_HID, AT_X = 0, 0, 0, 16, 0, 16, 32


def hybrid_layer(nc, x, mem, w_in, conv_w, conv_b, dt_bias, a_log, d_skip, norm_mix_w, ret_norm_w, ssd_norm_w,
                 w_ret_out, w_ssd_out, w_mix_out, norm_xa_w, mem_norm_w, w_xq, w_xkv, w_xo, norm_ff_w, w_ff1,
                 w_ff2, final_norm_w, consts, decay, merged_dram, nacs_dram, out):
    with ExitStack() as ctx:
        def sb(name, shape, dt=F32):
            return ctx.enter_context(nc.sbuf_tensor(name, shape, dt))

        def sem(name):
            return ctx.enter_context(nc.semaphore(name))

        raw = sb("raw", [P, RAW, CK * N])
        w_hi = sb("w_hi", [P, RING, CK * N], F32R)
        w_lo = sb("w_lo", [P, RING, CK * N], F32R)
        acts_hi = sb("acts_hi", [P, 48, T], F32R)
        acts_lo = sb("acts_lo", [P, 48, T], F32R)
        cst = sb("cst", [P, C_ALL])
        vec = sb("vec", [P, V_ALL])
        headrow = sb("headrow", [P, 3, SH])
        dtt = sb("dtt", [P, NT, SH])
        da = sb("da", [P, NT, SH])
        eacs = sb("eacs", [P, SH])
        dstate = sb("dstate", [P, SH])
        small = sb("small", [P, 128])
        reg_a = sb("reg_a", [P, 4096])
        reg_b = sb("reg_b", [P, 4096])
        reg_c = sb("reg_c", [P, 4096])
        nat = sb("nat", [P, NT, N])
        bcg = sb("bcg", [P, 2, T])
        junk = sb("junk", [P, N])

        acc = ctx.enter_context(nc.psum_tensor("acc", [P, 4 * N], F32))
        ptr = ctx.enter_context(nc.psum_tensor("ptr", [P, 2, N], F32))
        pss = ctx.enter_context(nc.psum_tensor("pss", [P, 2, N], F32))

        ident = cst[:, C_ID:C_ID + P]
        tri = cst[:, C_TRI:C_TRI + P]
        ones = cst[:, C_ONE:C_ONE + P]
        cos = cst[:, C_COS:C_COS + P].rearrange("p (t a d) -> p t a d", t=NT, a=1)
        sin = cst[:, C_SIN:C_SIN + P].rearrange("p (t a d) -> p t a d", t=NT, a=1)
        ss_x, rs_x = small[:, 0:2], small[:, 2:4]
        rs_mem = small[:, 6:8]
        ss_xa4, rs_xa = small[:, 8:16], small[:, 18:20]
        ss_ff4, rs_ff = small[:, 20:28], small[:, 30:32]
        rs_out, ss_out4 = small[:, 34:36], small[:, 112:120]
        ss_g, rs_g = small[:, 36:38], small[:, 38:40]
        mx, nmx, sm, rsm = small[:, 40:42], small[:, 42:44], small[:, 44:46], small[:, 46:48]
        bnst = small[:, 48:60].rearrange("p (t s) -> p t s", t=NT)
        bnag = small[:, 60:64]
        mv = small[:, 64:96]
        rgn = small[:, 96:112]
        stage = reg_b[:, 2048:2048 + 4 * P].rearrange("p (j n) -> p j n", j=4)
        dec_t = reg_c[:, 0:1024].rearrange("p (h i) -> p h i", h=HEADS)
        qkv = reg_c[:, 1024:2048].rearrange("p (t n) -> p t n", t=NT)
        rot_a = reg_c[:, 2048:2560].rearrange("p (t a d) -> p t a d", t=NT, a=4)
        rot_b = reg_c[:, 2560:3072].rearrange("p (t a d) -> p t a d", t=NT, a=4)
        rot = reg_c[:, 3072:3584].rearrange("p (t a d) -> p t a d", t=NT, a=4)
        rotm = reg_c[:, 3072:3584].rearrange("p (t a n) -> p t a n", t=NT, a=2)
        q_t, k_t = reg_c[:, 3584:3840], reg_c[:, 3840:4096]
        k_z = reg_a[:, 0:128]
        s_t = reg_a[:, 128:384].rearrange("p (c i) -> p c i", c=NT)
        kv_sb, cross_sb = reg_a[:, 384:640], reg_a[:, 640:896]
        y_ret = reg_b[:, :].rearrange("p (t n) -> p t n", t=NT)
        gated = reg_a[:, 0:1024].rearrange("p (t n) -> p t n", t=NT)
        sig_a = reg_c[:, :].rearrange("p (t n) -> p t n", t=NT)
        merged = sig_a
        bc_t = reg_a[:, :].rearrange("p (j n) -> p j n", j=16)
        conv = reg_b[:, 0:1024].rearrange("p (q n) -> p q n", q=4)
        xdtd = reg_b[:, 0:512]
        xs_n = reg_b[:, 1024:2048].rearrange("p (t n) -> p t n", t=NT)
        xdt = reg_b[:, 2048:3072].rearrange("p (t n) -> p t n", t=NT)
        y_ssd = reg_b[:, 3072:4096].rearrange("p (t n) -> p t n", t=NT)
        e_both = reg_c[:, 1024:3072].rearrange("p (c n) -> p c n", c=NT)
        e_m = [reg_c[:, 1024:2048], reg_c[:, 2048:3072]]
        s_z = reg_c[:, 3072:4096].rearrange("p (t n) -> p t n", t=NT)
        nacs = da[:, :, :]
        turned_dt = reg_b[0:SH, 3072:3072 + T]
        cbm = nat[:, 0, 0:2 * P].rearrange("p (c l) -> p c l", c=NT)
        cross = nat[:, 0, 2 * P:3 * P]
        hres = reg_a[:, :].rearrange("p (t n) -> p t n", t=NT)
        sig_b = reg_b[:, :].rearrange("p (t n) -> p t n", t=NT)
        mem_n = sig_b
        v_x = reg_c[:, :].rearrange("p (t n) -> p t n", t=NT)
        kx_t = reg_b[:, 0:1024].rearrange("p (q n) -> p q n", q=4)
        qx_t = reg_b[:, 1024:2048].rearrange("p (q n) -> p q n", q=4)
        prob = reg_b[:, 2048:2560].rearrange("p (t n) -> p t n", t=NT)
        prob_t = reg_b[:, 2560:3072]
        o_n = reg_b[:, 3072:4096].rearrange("p (t n) -> p t n", t=NT)
        sq_n = reg_b[:, 0:1024].rearrange("p (t n) -> p t n", t=NT)
        fnw = reg_c[:, 0:2048]

        w_landed = [sem(f"w_landed{s}") for s in range(RAW)]
        hi_ready = sem("hi_ready")
        lo_ready = sem("lo_ready")
        w_used = sem("w_used")
        acc_read = sem("acc_read")
        tp_done = sem("tp_done")
        tp_hi = sem("tp_hi")
        tp_read = sem("tp_read")
        in_x = [sem(f"in_x{j}") for j in range(4)]
        in_ident, in_cst, in_nm, in_vec, in_head, in_dec = (
            sem(n) for n in ("in_ident", "in_cst", "in_nm", "in_vec", "in_head", "in_dec"))
        in_mem = [sem(f"in_mem{j}") for j in range(2)]
        in_h, in_m, in_fn = (sem(n) for n in ("in_h", "in_m", "in_fn"))
        m_stored, out_stored = sem("m_stored"), sem("out_stored")
        vec_turned, vec_ready = sem("vec_turned"), sem("vec_ready")
        ss_done = sem("ss_done")
        var_done = sem("var_done")
        sqrt_done = sem("sqrt_done")
        rs_done = sem("rs_done")
        rotated, kz_ready, qk_turned, qk_copied = (sem(n) for n in ("rotated", "kz_ready", "qk_turned", "qk_copied"))
        scores_done, decayed, kv_copied = (sem(n) for n in ("scores_done", "decayed", "kv_copied"))
        inner_done, cross_copied, y_stored = (sem(n) for n in ("inner_done", "cross_copied", "y_stored"))
        gated_ready = sem("gated_ready")
        neg_abs_ready, exps_ready, one_plus_ready, ln_ready = (
            sem(n) for n in ("neg_abs_ready", "exps_ready", "one_plus_ready", "ln_ready"))
        da_ready, acs_done, acs_copied, ds_ready, ds_exp = (
            sem(n) for n in ("da_ready", "acs_done", "acs_copied", "ds_ready", "ds_exp"))
        tap_done = sem("tap_done")
        conv_done, bc_ready = sem("conv_done"), sem("bc_ready")
        xconv_done, xs_act, xdt_ready = sem("xconv_done"), sem("xs_act"), sem("xdt_ready")
        bcg_ready, cb_done, cross_ready = (sem(n) for n in ("bcg_ready", "cb_done", "cross_ready"))
        dt_copied, dt_turned, nacs_turned, nacs_copied, nacs_stored, in_nacs = (
            sem(n) for n in ("dt_copied", "dt_turned", "nacs_turned", "nacs_copied", "nacs_stored", "in_nacs"))
        seg_ready, exp_done, mt_ready = (sem(n) for n in ("seg_ready", "exp_done", "mt_ready"))
        ydiag_done, yoff_done = sem("ydiag_done"), sem("yoff_done")
        y_added, y_gated, gss_done, gvar_done, gsqrt_done, grs_done, y_ready = (
            sem(n) for n in ("y_added", "y_gated", "gss_done", "gvar_done", "gsqrt_done", "grs_done", "y_ready"))
        merged_ready, hg_ready, h_saved = sem("merged_ready"), sem("hg_ready"), sem("h_saved")
        xscores_done, nmx_ready, prob_ready, pt_done, pt_copied, pv_done, o_ready = (
            sem(n) for n in ("xscores_done", "nmx_ready", "prob_ready", "pt_done", "pt_copied", "pv_done", "o_ready"))
        sq_ready = sem("sq_ready")
        out_added, out_squared, out_gained, fin_act, fin_dve = (
            sem(n) for n in ("out_added", "out_squared", "out_gained", "fin_act", "fin_dve"))

        def need(eng, s, value):
            if isinstance(value, int) and value <= 0:
                return
            eng.wait_ge(s, value)

        def join(*parts):
            slots = {}
            for part in parts:
                for c, steps in part.items():
                    slots.setdefault(c, []).extend(steps)
            return slots

        def acc_of(i, t):
            if isinstance(i, int):
                return acc[:, (i % 2) * 2 * N + t * N:(i % 2) * 2 * N + (t + 1) * N]
            return acc[:, ds((i % 2) * (2 * N) + t * N, N)]

        def acc_both(i):
            if isinstance(i, int):
                a = acc[:, (i % 2) * 2 * N:(i % 2 + 1) * 2 * N]
            else:
                a = acc[:, ds((i % 2) * (2 * N), 2 * N)]
            return a.rearrange("p (t n) -> p t n", t=NT)

        def group_end(phase, i):
            return CHUNK[phase] + CPG[phase] * (i + 1)

        def landed(phase, slot, uses):
            if phase == "qkv":
                return 48 * uses
            return 16 * uses + 32 * (COUNT["qkv"] * CPG["qkv"] // RAW + (slot < LEAD))

        def tile_rows(w):
            return w.rearrange("(k p) n -> p k n", p=P)

        block = ctx.enter_context(nc.Block())

        @block.sync
        def _(sp):
            xv = x.rearrange("b (t p) n -> p (b t) n", p=P)

            def bring_x(j):
                sp.dma_start(hres[:, :, j * N:(j + 1) * N], xv[:, :, j * N:(j + 1) * N]).then_inc(in_x[j], 16)

            def bring(n, c, parts):
                need(sp, lo_ready, n - RAW + 1)
                for dst, src in parts:
                    sp.dma_start(dst, src).then_inc(w_landed[c % RAW], 16)

            def plain(phase, w, col, i, k_base=0, first=0):
                wv = tile_rows(w)
                for c in range(first, CPG[phase]):
                    dst = raw[:, c % RAW, :].rearrange("p (k n) -> p k n", k=CK)
                    bring(CHUNK[phase] + CPG[phase] * i + c, c,
                          [(dst, wv[:, k_base + c * CK:k_base + (c + 1) * CK, col])])

            wi = tile_rows(w_in[0])

            def heads_qkv(i):
                for c in range(CPG["qkv"]):
                    if isinstance(i, int) and c < 4:
                        bring_x(c)
                    dst = raw[:, c % RAW, :].rearrange("p (k n) -> p k n", k=CK)
                    kk = slice(c * CK, c * CK + CK)
                    qk = wi[:, kk, 0:2 * HEADS * DK].rearrange("p k (a n) -> p k a n", a=2)
                    need(sp, lo_ready, CHUNK["qkv"] + CPG["qkv"] * i + c - RAW + 1)
                    sp.dma_start(dst[:, :, 2 * DK:], wi[:, kk, ds(i * DV + V0, DV)]).then_inc(w_landed[c % RAW], 16)
                    for k in range(CK):
                        sp.dma_start(dst[:, k, 0:2 * DK].rearrange("p (a n) -> p a n", a=2),
                                     qk[:, k, :, ds(i * DK, DK)]).then_inc(w_landed[c % RAW], 16)

            heads_qkv(0)
            with sp.Fori(1, HEADS) as i:
                heads_qkv(i)
            for c in range(LEAD):
                dst = raw[:, c % RAW, :].rearrange("p (k n) -> p k n", k=CK)
                bring(CHUNK["gate"] + c, c, [(dst[:, 0, 0:N // 2], wi[:, CK * c, G0:G0 + N // 2]),
                                             (dst[:, 0, N // 2:], wi[:, CK * c, G0 + N // 2:G0 + N]),
                                             (dst[:, 1, :], wi[:, CK * c + 1, G0:G0 + N])])
            plain("gate", w_in[0], slice(G0, G0 + N), 0, first=LEAD)
            with sp.Fori(1, 4) as i:
                plain("gate", w_in[0], ds(i * N + G0, N), i)
            with sp.Fori(0, 4) as i:
                plain("sig_a", w_in[0], ds(i * N + GA0, N), i)
            with sp.Fori(0, 4) as i:
                plain("ret_out", w_ret_out[0], ds(i * N, N), i)
            for c in range(CPG["dt"]):
                dst = raw[:, c % RAW, 0:4 * SH].rearrange("p (k n) -> p k n", k=4)
                bring(CHUNK["dt"] + c, c, [(dst, wi[:, 4 * c:4 * c + 4, DT0:DT0 + SH])])
            with sp.Fori(0, 4) as i:
                plain("bc", w_in[0], ds(i * N + B0, N), i)
            with sp.Fori(0, SG) as g:
                plain("xz", w_in[0], ds(g * N + X0, N), g * 2)
                plain("xz", w_in[0], ds(g * N + Z0, N), g * 2 + 1)
            with sp.Fori(0, 4) as i:
                plain("sig_b", w_in[0], ds(i * N + GB0, N), i)
            with sp.Fori(0, 4) as i:
                plain("ssd_out", w_ssd_out[0], ds(i * N, N), i)
            with sp.Fori(0, 4) as i:
                plain("mix", w_mix_out[0], ds(i * N, N), i)
            with sp.Fori(0, 4) as i:
                plain("xv", w_xkv[0], ds(i * N + D, N), i)
            with sp.Fori(0, XH) as i:
                plain("kq", w_xkv[0], ds(i * N, N), i * 2)
                plain("kq", w_xq[0], ds(i * N, N), i * 2 + 1)
            with sp.Fori(0, 4) as i:
                plain("xo", w_xo[0], ds(i * N, N), i)
            for half, (up, down) in enumerate((("ff1a", "ff2a"), ("ff1b", "ff2b"))):
                with sp.Fori(0, 8) as i:
                    plain(up, w_ff1[0], ds(i * N + half * (FF // 2), N), i)
                with sp.Fori(0, 4) as i:
                    plain(down, w_ff2[0], ds(i * N, N), i, k_base=half * (FF // 2 // P))
            ov = out.rearrange("b (t p) n -> p (b t) n", p=P)
            for t in range(NT):
                for s, cols in ((fin_dve, slice(D // 2, D)), (fin_act, slice(0, D // 2))):
                    sp.wait_ge(s, t + 1)
                    sp.dma_start(ov[:, t, cols], hres[:, t, cols]).then_inc(out_stored, 16)
            sp.wait_ge(out_stored, 32 * NT)

        @block.gpsimd
        def _(pool):
            for v, w in ((V_XA, norm_xa_w), (V_MEM, mem_norm_w), (V_FF, norm_ff_w),
                         (V_RET, ret_norm_w), (V_SSD, ssd_norm_w)):
                n = w.shape[1] // P
                pool.dma_start(stage[v:v + n, 0, :], w[0].rearrange("(j p) -> j p", p=P)).then_inc(in_vec, 16)
            pool.dma_start(stage[0:48, 1, :], conv_b[0].rearrange("(j p) -> j p", p=P)).then_inc(in_vec, 16)
            cw = conv_w[0].rearrange("k (j p) -> (k j) p", p=P)
            for h in range(2):
                pool.dma_start(stage[0:96, 2 + h, :], cw[96 * h:96 * h + 96, :]).then_inc(in_vec, 16)
            for j, w in enumerate((dt_bias, a_log, d_skip)):
                pool.dma_start(headrow[:, j, :], w.partition_broadcast(P)[:, 0, :]).then_inc(in_head, 16)
            pool.dma_start(dec_t, decay.rearrange("p (h i) -> p h i", h=HEADS)).then_inc(in_dec, 16)
            pool.wait_ge(acc_read, GROUP["ret_out"] + 4)
            pool.dma_start(merged_dram.rearrange("p (t n) -> p t n", t=NT), merged).then_inc(m_stored, 16)
            pool.wait_ge(nacs_copied, 1)
            pool.dma_start(nacs_dram.rearrange("c (h l) -> h c l", h=SH),
                           turned_dt.rearrange("p (c l) -> p c l", c=NT)).then_inc(nacs_stored, 16)
            pool.wait_ge(bc_ready, 4)
            pool.wait_ge(nacs_stored, 16)
            pool.wait_ge(m_stored, 16)
            with pool.Fori(0, SG) as g:
                need(pool, yoff_done, g)
                pool.tensor_copy(bcg[:, 0, :], bc_t[:, ds(g, 1), :].rearrange("p a n -> p (a n)"))
                pool.tensor_copy(bcg[:, 1, :], bc_t[:, ds(g + SG, 1), :].rearrange("p a n -> p (a n)")) \
                    .then_inc(bcg_ready, 1)
                need(pool, ydiag_done, g * 2)
                pool.dma_start(e_both, nacs_dram[:, ds(g * (RH * P), RH * P)].partition_broadcast(P)) \
                    .then_inc(in_nacs, 16)
            pool.wait_ge(tp_read, PACKS["xz"] + 48)
            pool.wait_ge(m_stored, 16)
            xv = x.rearrange("b (t p) n -> p (b t) n", p=P)
            pool.dma_start(merged, merged_dram.rearrange("p (t n) -> p t n", t=NT)).then_inc(in_m, 16)
            pool.dma_start(hres, xv).then_inc(in_h, 16)
            pool.wait_ge(merged_ready, 4)
            mem_v = mem.rearrange("b (t p) n -> p (b t) n", p=P)
            for j in range(2):
                half = slice(j * (D // 2), (j + 1) * (D // 2))
                pool.dma_start(mem_n[:, :, half], mem_v[:, :, half]).then_inc(in_mem[j], 16)
            pool.wait_ge(pv_done, XH)
            pool.dma_start(fnw, final_norm_w.partition_broadcast(P)).then_inc(in_fn, 16)

        @block.tensor
        def _(pe):
            def turn(dst, src):
                return pe.transpose(dst, src, ident)

            def pack_start(m):
                need(pe, tp_read, m - 1)

            def split_pack(m, b, cols):
                pack_start(m)
                for k in range(2):
                    for t in range(NT):
                        last = turn(ptr[:, b, k * T + t * P:k * T + (t + 1) * P], cols(k, t))
                last.then_inc(tp_done, 1)

            def gemm(phase, i, at, hooks, parity=None, ready=None, lhs_at=0):
                par = i if parity is None else parity
                n0 = CHUNK[phase] + CPG[phase] * i
                need(pe, acc_read, GROUP[phase] + i - 1)
                for c in range(CPG[phase]):
                    if ready and c in ready:
                        pe.wait_ge(tp_read, ready[c])
                    need(pe, lo_ready, n0 + c + 1)
                    for k in range(CK):
                        kt = c * CK + k
                        for t in range(NT):
                            xh = acts_hi[:, at + kt, t * P:(t + 1) * P]
                            xl = acts_lo[:, at + kt, t * P:(t + 1) * P]
                            wh = w_hi[:, c % RING, k * N:(k + 1) * N]
                            wl = w_lo[:, c % RING, k * N:(k + 1) * N]
                            o = acc_of(par, t)
                            pe.matmul(o, xh, wh, start=kt == 0, stop=False)
                            pe.matmul(o, xh, wl, start=False, stop=False)
                            last = pe.matmul(o, xl, wh, start=False, stop=kt == CPG[phase] * CK - 1)
                    last.then_inc(w_used, 1)
                    for step in hooks.get(c, ()):
                        step()

            pe.wait_ge(in_ident, 16)
            pe.wait_ge(in_nm, 16)
            pe.transpose(pss[:, 0, 0:KT], stage[0:KT, 0, :], ident[0:KT, 0:KT]).then_inc(vec_turned, 1)

            def x_pack(m):
                if m % 2 == 0:
                    pe.wait_ge(in_x[m // 2], 16)
                split_pack(PACKS["x"] + m, m % 2, lambda k, t: hres[:, t, (2 * m + k) * P:(2 * m + k + 1) * P])

            def other_vectors():
                pe.wait_ge(in_cst, 16)
                pe.wait_ge(in_vec, 128)
                pe.wait_ge(vec_ready, 1)
                for j, (r, v) in enumerate(((112, 0), (48, V_CB), (96, V_CW), (96, V_CW + 96))):
                    last = pe.transpose(pss[:, 0, v:v + r], stage[0:r, j, :], ident[0:r, 0:r])
                last.then_inc(vec_turned, 1)

            for m in range(2):
                x_pack(m)

            def qk_turn(i):
                pe.wait_ge(rotated, i + 1)
                need(pe, qk_copied, i)
                if isinstance(i, int) and i == 0:
                    pe.wait_ge(vec_ready, 2)
                for a in range(2):
                    for t in range(NT):
                        last = turn(pss[:, 0, a * T + t * P:a * T + (t + 1) * P], rotm[:, t, a, :])
                last.then_inc(qk_turned, 1)

            def ret_scores(i):
                pe.wait_ge(qk_copied, i + 1)
                pe.wait_ge(kz_ready, i + 1)
                need(pe, decayed, i)
                need(pe, kv_copied, i)
                for c in range(NT):
                    pe.matmul(pss[:, 1, c * P:(c + 1) * P], k_t[:, c * P:(c + 1) * P], q_t[:, c * P:(c + 1) * P],
                              start=True, stop=True)
                pe.matmul(pss[:, 1, T:T + DV], k_z, qkv[:, 0, 2 * DK:], start=True, stop=True) \
                    .then_inc(scores_done, 1)

            def ret_inner(i):
                pe.wait_ge(decayed, i + 1)
                pe.wait_ge(kv_copied, i + 1)
                need(pe, y_stored, i)
                for c in range(NT):
                    pe.matmul(ptr[:, 0, c * DV:(c + 1) * DV], s_t[:, c, :], qkv[:, c, 2 * DK:],
                              start=True, stop=True)
                pe.matmul(ptr[:, 1, 0:DV], q_t[:, P:2 * P], kv_sb, start=True, stop=True).then_inc(inner_done, 1)

            def retention(i):
                return {1: [lambda: qk_turn(i)], 3: [lambda: ret_scores(i)], 5: [lambda: ret_inner(i)]}

            gemm("qkv", 0, AT_X, join({0: [lambda: x_pack(2)], 5: [other_vectors]},
                                    {c: [lambda m=c + 3: x_pack(m)] for c in range(5)}),
                 ready={c: PACKS["x"] + c + 1 for c in range(8)})
            with pe.Fori(1, HEADS) as i:
                gemm("qkv", i, AT_X, retention(i - 1))

            def gate_packs(i):
                pe.wait_ge(gated_ready, i + 1)
                for j in range(2):
                    split_pack(PACKS["gate"] + 2 * i + j, j,
                               lambda k, t: gated[:, t, (2 * j + k) * P:(2 * j + k + 1) * P])

            def gate(i):
                return {2: [lambda: gate_packs(i)]}

            gemm("gate", 0, AT_X, retention(HEADS - 1))
            with pe.Fori(1, 4) as i:
                gemm("gate", i, AT_X, gate(i - 1))
            gemm("sig_a", 0, AT_X, gate(3))
            with pe.Fori(1, 4) as i:
                gemm("sig_a", i, AT_X, {})
            gemm("ret_out", 0, AT_RET, {}, ready={0: PACKS["gate"] + 8})
            with pe.Fori(1, 4) as i:
                gemm("ret_out", i, AT_RET, {})

            for c in range(CPG["dt"]):
                pe.wait_ge(lo_ready, CHUNK["dt"] + c + 1)
                for k in range(4):
                    kt = c * 4 + k
                    xh, xl = acts_hi[:, AT_X + kt, :], acts_lo[:, AT_X + kt, :]
                    wh = w_hi[:, c % RING, k * SH:(k + 1) * SH]
                    wl = w_lo[:, c % RING, k * SH:(k + 1) * SH]
                    o = pss[0:SH, 0, 0:T]
                    pe.matmul(o, wh, xh, start=kt == 0, stop=False)
                    pe.matmul(o, wl, xh, start=False, stop=False)
                    last = pe.matmul(o, wh, xl, start=False, stop=kt == KT - 1)
                last.then_inc(w_used, 1)

            def dt_turn():
                pe.wait_ge(dt_copied, 1)
                for t in range(NT):
                    last = pe.transpose(pss[:, 1, t * SH:(t + 1) * SH], turned_dt[:, t * P:(t + 1) * P],
                                        ident[0:SH, 0:SH])
                last.then_inc(dt_turned, 1)

            def dt_sums():
                pe.wait_ge(da_ready, 1)
                for t in range(NT):
                    pe.matmul(pss[:, 0, t * SH:(t + 1) * SH], tri, da[:, t, :], start=True, stop=True)
                pe.matmul(pss[:, 0, 2 * SH:3 * SH], ones, da[:, 0, :], start=True, stop=True).then_inc(acs_done, 1)

            def nacs_turn():
                pe.wait_ge(acs_copied, 1)
                for t in range(NT):
                    last = turn(pss[0:SH, 1, t * P:(t + 1) * P], nacs[:, t, :])
                last.then_inc(nacs_turned, 1)

            def nat_packs(m):
                for j in range(2):
                    split_pack(m + j, j, lambda k, t: nat[:, t, (2 * j + k) * P:(2 * j + k + 1) * P])

            def bc_turn(i):
                pe.wait_ge(acc_read, GROUP["bc"] + i + 1)
                nat_packs(PACKS["bc"] + 2 * i)

            gemm("bc", 0, AT_X, {0: [dt_turn], 7: [dt_sums]})
            gemm("bc", 1, AT_X, {1: [lambda: bc_turn(0)], 2: [nacs_turn]})
            with pe.Fori(2, 4) as i:
                gemm("bc", i, AT_X, {1: [lambda: bc_turn(i - 1)]})

            def xs_turn(g):
                pe.wait_ge(acc_read, GROUP["xz"] + 2 * g + 1)
                nat_packs(PACKS["xz"] + 6 * g)

            def xs_back(g):
                pe.wait_ge(xs_act, 2 * g + 2)
                for t in range(NT):
                    pack_start(PACKS["xz"] + 6 * g + 2 + t)
                    for q in range(4):
                        last = turn(ptr[:, t, q * P:(q + 1) * P], conv[:, q, t * P:(t + 1) * P])
                    last.then_inc(tp_done, 1)

            def ssd_cb(g):
                pe.wait_ge(bcg_ready, g + 1)
                pe.wait_ge(tp_read, PACKS["xz"] + 6 * g + 4)
                pe.matmul(ptr[:, 0, 0:T], bcg[:, 0, 0:P], bcg[:, 1, :], start=True, stop=True)
                pe.matmul(ptr[:, 0, T:T + P], bcg[:, 0, P:T], bcg[:, 1, P:T], start=True, stop=True) \
                    .then_inc(cb_done, 1)

            def ssd_diag(g, c):
                pe.wait_ge(mt_ready, 2 * g + c + 1)
                need(pe, y_added, 3 * g)
                for r in range(RH):
                    last = pe.matmul(pss[:, c, r * SP_:(r + 1) * SP_], e_m[c][:, r * P:(r + 1) * P],
                                     xdt[:, c, r * SP_:(r + 1) * SP_], start=True, stop=True)
                last.then_inc(ydiag_done, 1)

            def ssd_off(g):
                pe.wait_ge(cross_ready, g + 1)
                pe.wait_ge(xdt_ready, g + 1)
                pe.matmul(ptr[:, 1, :], cross, xdtd, start=True, stop=True).then_inc(yoff_done, 1)

            def ssd_packs(g):
                pe.wait_ge(y_ready, g + 1)
                for j in range(2):
                    split_pack(PACKS["xz"] + 6 * g + 4 + j, j,
                               lambda k, t: y_ssd[:, t, (2 * j + k) * P:(2 * j + k + 1) * P])

            def during_z(g):
                return {2: [lambda: xs_turn(g)], 6: [lambda: xs_back(g)]}

            def during_xs(g):
                return {0: [lambda: ssd_cb(g)], 2: [lambda: ssd_off(g)], 3: [lambda: ssd_diag(g, 0)],
                        4: [lambda: ssd_diag(g, 1)]}

            gemm("xz", 0, AT_X, {1: [lambda: bc_turn(3)]}, parity=0)
            gemm("xz", 1, AT_X, during_z(0), parity=1)
            with pe.Fori(1, SG) as g:
                gemm("xz", g * 2, AT_X, during_xs(g - 1), parity=0)
                gemm("xz", g * 2 + 1, AT_X, join({0: [lambda: ssd_packs(g - 1)]}, during_z(g)), parity=1)

            gemm("sig_b", 0, AT_X, during_xs(SG - 1))
            gemm("sig_b", 1, AT_X, {0: [lambda: ssd_packs(SG - 1)]})
            with pe.Fori(2, 4) as i:
                gemm("sig_b", i, AT_X, {})

            def merge_turn(i):
                pe.wait_ge(merged_ready, i + 1)
                nat_packs(PACKS["ssd_out"] + 2 * i)

            gemm("ssd_out", 0, AT_SSD, {}, ready={0: PACKS["xz"] + 48})
            with pe.Fori(1, 4) as i:
                gemm("ssd_out", i, AT_SSD, {4: [lambda: merge_turn(i - 1)]})

            def mem_packs(lo, hi):
                for m in range(lo, hi):
                    if m % 4 == 0:
                        pe.wait_ge(in_mem[m // 4], 16)
                    split_pack(PACKS["mem"] + m, m % 2,
                               lambda k, t: mem_n[:, t, (2 * m + k) * P:(2 * m + k + 1) * P])

            def h_turn(phase, base, i):
                pe.wait_ge(hg_ready, base + i + 1)
                nat_packs(PACKS[phase] + 2 * i)

            gemm("mix", 0, AT_X, {2: [lambda: merge_turn(3)], 4: [lambda: mem_packs(0, 2)],
                                  5: [lambda: mem_packs(2, 4)], 6: [lambda: mem_packs(4, 6)],
                                  7: [lambda: mem_packs(6, 8)]},
                 ready={0: PACKS["ssd_out"] + 6, 6: PACKS["ssd_out"] + 8})
            with pe.Fori(1, 4) as i:
                gemm("mix", i, AT_X, {1: [lambda: h_turn("mix", 0, i - 1)]})

            gemm("xv", 0, AT_MEM, {1: [lambda: h_turn("mix", 0, 3)]})
            with pe.Fori(1, 4) as i:
                gemm("xv", i, AT_MEM, {})

            def k_turn(n):
                pe.wait_ge(acc_read, GROUP["kq"] + 2 * n + 1)
                nat_packs(PACKS["kq"] + 6 * n)

            def q_turn(n):
                pe.wait_ge(acc_read, GROUP["kq"] + 2 * n + 2)
                nat_packs(PACKS["kq"] + 6 * n + 2)

            def x_scores(n):
                pe.wait_ge(tp_read, PACKS["kq"] + 6 * n + 4)
                for t in range(NT):
                    for q in range(4):
                        last = pe.matmul(pss[:, 0, t * T:(t + 1) * T], qx_t[:, q, t * P:(t + 1) * P],
                                         kx_t[:, q, :], start=q == 0, stop=q == 3)
                last.then_inc(xscores_done, 1)

            def p_turn(n):
                pe.wait_ge(prob_ready, n + 1)
                for m in range(NT):
                    for t in range(NT):
                        last = turn(pss[:, 1, m * T + t * P:m * T + (t + 1) * P], prob[:, t, m * P:(m + 1) * P])
                last.then_inc(pt_done, 1)

            def p_v(n):
                pe.wait_ge(pt_copied, n + 1)
                for t in range(NT):
                    for m in range(NT):
                        v = v_x[:, m, n * N:(n + 1) * N] if isinstance(n, int) else v_x[:, m, ds(n * N, N)]
                        last = pe.matmul(pss[:, t, :], prob_t[:, m * T + t * P:m * T + (t + 1) * P], v,
                                         start=m == 0, stop=m == 1)
                last.then_inc(pv_done, 1)

            def o_packs(n):
                pe.wait_ge(o_ready, n + 1)
                for j in range(2):
                    split_pack(PACKS["kq"] + 6 * n + 4 + j, j,
                               lambda k, t: o_n[:, t, (2 * j + k) * P:(2 * j + k + 1) * P])

            def attention(n):
                return {0: [lambda: q_turn(n)], 1: [lambda: x_scores(n)], 2: [lambda: p_turn(n)],
                        3: [lambda: p_v(n)], 4: [lambda: o_packs(n)]}

            gemm("kq", 0, AT_MEM, {}, parity=0)
            gemm("kq", 1, AT_XA, {1: [lambda: k_turn(0)]}, parity=1, ready={0: PACKS["mix"] + 8})
            with pe.Fori(1, XH) as n:
                gemm("kq", n * 2, AT_MEM, attention(n - 1), parity=0)
                gemm("kq", n * 2 + 1, AT_XA, {1: [lambda: k_turn(n)]}, parity=1)
            gemm("xo", 0, AT_X, attention(XH - 1),
                 ready={0: PACKS["kq"] + 18, 6: PACKS["kq"] + 24})
            with pe.Fori(1, 4) as i:
                gemm("xo", i, AT_X, {1: [lambda: h_turn("xo", 4, i - 1)]})

            def sq_turn(phase, i):
                b = 8 if phase == "ff1b" else 0
                pe.wait_ge(sq_ready, b + i + 1)
                for j in range(2):
                    split_pack(PACKS[phase] + 2 * i + j, j,
                               lambda k, t: sq_n[:, t, (2 * j + k) * P:(2 * j + k + 1) * P])

            for up, down in (("ff1a", "ff2a"), ("ff1b", "ff2b")):
                if up == "ff1a":
                    gemm(up, 0, AT_FF, {1: [lambda: h_turn("xo", 4, 3)]},
                         ready={0: PACKS["xo"] + 6, 6: PACKS["xo"] + 8})
                else:
                    gemm(up, 0, AT_FF, {})
                with pe.Fori(1, 8) as i:
                    gemm(up, i, AT_FF, {1: [lambda: sq_turn(up, i - 1)]})
                gemm(down, 0, AT_HID, {1: [lambda: sq_turn(up, 7)]},
                     ready={0: PACKS[up] + 14, 14: PACKS[up] + 16})
                with pe.Fori(1, 4) as i:
                    gemm(down, i, AT_HID, {})

        @block.scalar
        def _(act):
            def copy(o, i, scale=1.0):
                return act.activation(o, i, ACT.Copy, scale=scale)

            def split_hi(phase, i, c):
                n = CHUNK[phase] + CPG[phase] * i + c + LEAD
                s = (c + LEAD) % RAW
                uses = CHUNK[phase] // RAW + (CPG[phase] // RAW) * i + (c + LEAD) // RAW + 1
                act.wait_ge(w_landed[s], landed(phase, s, uses))
                need(act, w_used, n - RING + 1)
                copy(w_hi[:, s, :], raw[:, s, :]).then_inc(hi_ready, 1)

            def slots(phase, i, hooks, final=False):
                for c in range(CPG[phase]):
                    if not (final and c + LEAD >= CPG[phase]):
                        split_hi(phase, i, c)
                    for step in hooks.get(c, ()):
                        step()

            def group_ready(phase, i):
                act.wait_ge(w_used, group_end(phase, i))
                need(act, acc_read, GROUP[phase] + i)

            def hi_pack(phase, m, b, at, col=None, sp_=None):
                act.wait_ge(tp_done, PACKS[phase] + m + 1)
                if col is None:
                    o = acts_hi[:, at:at + 2, :] if isinstance(at, int) else acts_hi[:, ds(at, 2), :]
                    copy(o, ptr[:, b, :].rearrange("p (k n) -> p k n", k=2)).then_inc(tp_hi, 1)
                    return
                for k in range(2):
                    a, v = at + k, col + k
                    o = acts_hi[:, a, :] if isinstance(a, int) else \
                        acts_hi[:, ds(a, 1), :].rearrange("p a n -> p (a n)")
                    sc = vec[:, v:v + 1] if isinstance(v, int) else vec[:, ds(v, 1)]
                    last = copy(o, ptr[:, b, k * T:(k + 1) * T], sc)
                last.then_inc(tp_hi, 1)

            act.dma_start(ident, consts[:, 0:P]).then_inc(in_ident, 16)
            act.dma_start(stage[0:KT, 0, :], norm_mix_w[0].rearrange("(j p) -> j p", p=P)).then_inc(in_nm, 16)
            act.dma_start(cst[:, P:], consts[:, P:]).then_inc(in_cst, 16)

            def x_hi(m):
                hi_pack("x", m, m % 2, AT_X + 2 * m, V_MIX + 2 * m)

            for n in range(LEAD):
                act.wait_ge(w_landed[n], landed("qkv", n, 1))
                copy(w_hi[:, n, :], raw[:, n, :]).then_inc(hi_ready, 1)
                if n == 0:
                    act.wait_ge(vec_ready, 1)
                if n < 2:
                    x_hi(n)

            def x_squares(t):
                act.drain()
                act.activation(reg_b[:, 0:D], hres[:, t, :], ACT.Square, accum_out=ss_x[:, t:t + 1]) \
                    .then_inc(ss_done, 1)

            def root(n, v):
                act.wait_ge(var_done, n)
                act.activation(v, v, ACT.Sqrt).then_inc(sqrt_done, 1)

            def qkv_copy(i):
                group_ready("qkv", i)
                need(act, inner_done, i)
                need(act, rotated, i)
                for t in range(NT):
                    last = copy(qkv[:, t, :], acc_of(i, t), rs_x[:, t:t + 1])
                last.then_inc(acc_read, 1)

            def qk_copy(i):
                act.wait_ge(qk_turned, i + 1)
                copy(q_t, pss[:, 0, 0:T], DK ** -0.5)
                copy(k_t, pss[:, 0, T:2 * T]).then_inc(qk_copied, 1)

            def kv_copy(i):
                act.wait_ge(scores_done, i + 1)
                act.wait_ge(decayed, i + 1)
                copy(kv_sb, pss[:, 1, T:T + DV]).then_inc(kv_copied, 1)

            def cross_copy(i):
                act.wait_ge(inner_done, i + 1)
                need(act, y_stored, i)
                xi = cst[:, C_XI + i:C_XI + i + 1] if isinstance(i, int) else cst[:, ds(i + C_XI, 1)]
                copy(cross_sb, ptr[:, 1, 0:DV], xi).then_inc(cross_copied, 1)

            def retention(i):
                return {0: [lambda: qkv_copy(i)], 2: [lambda: qk_copy(i)], 4: [lambda: kv_copy(i)],
                        6: [lambda: cross_copy(i)]}

            slots("qkv", 0, {0: [lambda: x_hi(2), lambda: x_hi(3)], **{c: [lambda m=c + 2: x_hi(m)] for c in (2, 3, 4)},
                             5: [lambda: x_hi(7), lambda: x_squares(0)], 6: [lambda: x_squares(1)],
                             7: [lambda: root(1, rs_x), lambda: act.wait_ge(rs_done, 1)]})
            with act.Fori(1, HEADS) as i:
                slots("qkv", i, retention(i - 1))

            def gate_silu(i):
                group_ready("gate", i)
                need(act, tp_done, PACKS["gate"] + 2 * i)
                for t in range(NT):
                    last = act.activation(gated[:, t, :], acc_of(i, t), ACT.Silu, scale=rs_x[:, t:t + 1])
                last.then_inc(acc_read, 1)

            def gate_hi(i):
                for j in range(2):
                    hi_pack("gate", 2 * i + j, j, 4 * i + (AT_RET + 2 * j), 4 * i + (V_RET + 2 * j))

            def gate(i):
                return {0: [lambda: gate_silu(i)], 3: [lambda: gate_hi(i)]}

            slots("gate", 0, {**retention(HEADS - 1), 7: [lambda: root(2, rgn)]})
            with act.Fori(1, 4) as i:
                slots("gate", i, gate(i - 1))

            def sig_to(phase, i, dst):
                group_ready(phase, i)
                for t in range(NT):
                    o = dst[:, t, i * N:(i + 1) * N] if isinstance(i, int) else dst[:, t, ds(i * N, N)]
                    last = act.activation(o, acc_of(i, t), ACT.Sigmoid, scale=rs_x[:, t:t + 1])
                last.then_inc(acc_read, 1)

            slots("sig_a", 0, gate(3))
            with act.Fori(1, 4) as i:
                slots("sig_a", i, {1: [lambda: sig_to("sig_a", i - 1, sig_a)]})
            slots("ret_out", 0, {1: [lambda: sig_to("sig_a", 3, sig_a)]})
            with act.Fori(1, 4) as i:
                slots("ret_out", i, {})
            slots("dt", 0, {})

            wk = junk[:, :].rearrange("p (a t n) -> p a t n", a=4, t=NT)

            def dt_copy():
                act.wait_ge(w_used, CHUNK["dt"] + CPG["dt"])
                copy(turned_dt, pss[0:SH, 0, 0:T]).then_inc(dt_copied, 1)

            def dt_exp():
                act.wait_ge(neg_abs_ready, 1)
                act.activation(wk[:, 1], wk[:, 1], ACT.Exp).then_inc(exps_ready, 1)
                act.activation(headrow[:, 1, :], headrow[:, 1, :], ACT.Exp).then_inc(exps_ready, 1)

            def dt_ln():
                act.wait_ge(one_plus_ready, 1)
                act.activation(wk[:, 3], wk[:, 2], ACT.Ln).then_inc(ln_ready, 1)

            def acs_copy():
                act.wait_ge(acs_done, 1)
                copy(nacs, pss[:, 0, 0:2 * SH].rearrange("p (t h) -> p t h", t=NT), -1.0)
                copy(junk[:, 0:SH], pss[:, 0, 2 * SH:3 * SH])
                act.activation(eacs[:, :], pss[:, 0, SH:2 * SH], ACT.Exp).then_inc(acs_copied, 1)

            def ds_exp_():
                act.wait_ge(ds_ready, 1)
                act.activation(dstate[:, :], dstate[:, :], ACT.Exp).then_inc(ds_exp, 1)

            def nat_copy(phase, i, m, scale, parity=None):
                group_ready(phase, i)
                need(act, tp_done, m)
                for t in range(NT):
                    last = copy(nat[:, t, :], acc_of(i if parity is None else parity, t), scale[:, t:t + 1])
                last.then_inc(acc_read, 1)

            def conv_tap(phase, m, b, q0, ct):
                act.wait_ge(tp_done, PACKS[phase] + m + 1)
                for k in range(2):
                    w, v = ct + (V_CW + 3 * (CONV // P) + k), ct + (V_CB + k)
                    w = vec[:, w:w + 1] if isinstance(w, int) else vec[:, ds(w, 1)]
                    v = vec[:, v:v + 1] if isinstance(v, int) else vec[:, ds(v, 1)]
                    last = act.activation(conv[:, q0 + k, :], ptr[:, b, k * T:(k + 1) * T], ACT.Identity,
                                          bias=v, scale=w)
                last.then_inc(tap_done, 1)

            def bc_taps(i):
                for j in range(2):
                    conv_tap("bc", 2 * i + j, j, 2 * j, i * 4 + (INNER // P + 2 * j))

            def bc_silu(i):
                act.wait_ge(conv_done, i + 1)
                o = bc_t[:, 4 * i:4 * i + 4, :] if isinstance(i, int) else bc_t[:, ds(i * 4, 4), :]
                act.activation(o, conv, ACT.Silu).then_inc(bc_ready, 1)

            def bc(i):
                return {0: [lambda: nat_copy("bc", i, PACKS["bc"] + 2 * i, rs_x)], 3: [lambda: bc_taps(i)],
                        7: [lambda: bc_silu(i)]}

            def nacs_copy():
                act.wait_ge(nacs_turned, 1)
                copy(turned_dt, pss[0:SH, 1, 0:T]).then_inc(nacs_copied, 1)

            slots("bc", 0, {0: [dt_copy], 1: [dt_exp], 3: [dt_ln]})
            slots("bc", 1, join(bc(0), {0: [acs_copy], 2: [ds_exp_], 3: [nacs_copy]}))
            with act.Fori(2, 4) as i:
                slots("bc", i, bc(i - 1))

            def xs_copy(g):
                need(act, mt_ready, 2 * g)
                need(act, yoff_done, g)
                if isinstance(g, int) and g == 0:
                    nat_copy("xz", 0, PACKS["bc"] + 8, rs_x, parity=0)
                else:
                    nat_copy("xz", g * 2, g * 6 + (PACKS["xz"] - 4), rs_x, parity=0)

            def xs_tap(g, j):
                need(act, yoff_done, g)
                conv_tap("xz", 6 * g + j, j, 2 * j, g * 4 + 2 * j)

            def xs_silu(g, j):
                act.wait_ge(xconv_done, 2 * g + j + 1)
                half = conv[:, 2 * j:2 * j + 2, :]
                act.activation(half, half, ACT.Silu).then_inc(xs_act, 1)

            def xs_nat(g):
                need(act, xdt_ready, g)
                for t in range(NT):
                    act.wait_ge(tp_done, PACKS["xz"] + 6 * g + 3 + t)
                    copy(xs_n[:, t, :], ptr[:, t, :]).then_inc(tp_read, 1)

            def z_silu(g):
                group_ready("xz", 2 * g + 1)
                need(act, y_gated, g)
                for t in range(NT):
                    last = act.activation(s_z[:, t, :], acc_of(1, t), ACT.Silu, scale=rs_x[:, t:t + 1])
                last.then_inc(acc_read, 1)

            def cross_cb(g):
                act.wait_ge(cb_done, g + 1)
                copy(cross, ptr[:, 0, P:T]).then_inc(cross_ready, 1)

            def seg_exp(g, c):
                act.wait_ge(seg_ready, 2 * g + c + 1)
                for r in range(RH):
                    b = nacs[:, c, g * RH + r:g * RH + r + 1] if isinstance(g, int) else \
                        nacs[:, c, ds(g * RH + r, 1)]
                    e = e_m[c][:, r * P:(r + 1) * P]
                    last = act.activation(e, e, ACT.Exp, bias=b, scale=-1.0)
                last.then_inc(exp_done, 1)

            def y_squares(g):
                act.wait_ge(y_gated, g + 1)
                for t in range(NT):
                    last = act.activation(junk[:, :], y_ssd[:, t, :], ACT.Square, accum_out=ss_g[:, t:t + 1])
                    act.drain() if t == 0 else None
                last.then_inc(gss_done, 1)

            def y_root(g):
                act.wait_ge(gvar_done, g + 1)
                act.activation(rs_g, rs_g, ACT.Sqrt).then_inc(gsqrt_done, 1)

            def y_scale(g):
                act.wait_ge(grs_done, g + 1)
                for t in range(NT):
                    last = copy(y_ssd[:, t, :], y_ssd[:, t, :], rs_g[:, t:t + 1])
                last.then_inc(y_ready, 1)

            def ssd_hi(g):
                for j in range(2):
                    hi_pack("xz", 6 * g + 4 + j, j, 4 * g + (AT_SSD + 2 * j), 4 * g + (V_SSD + 2 * j))

            def during_z(g):
                return {1: [lambda: xs_copy(g)], 3: [lambda: xs_tap(g, 0), lambda: xs_tap(g, 1)],
                        5: [lambda: xs_silu(g, 0)], 6: [lambda: xs_silu(g, 1)], 7: [lambda: xs_nat(g)]}

            def during_xs(g):
                return {0: [lambda: z_silu(g)], 1: [lambda: cross_cb(g), lambda: seg_exp(g, 0)],
                        2: [lambda: seg_exp(g, 1)], 6: [lambda: y_squares(g)],
                        7: [lambda: y_root(g)]}

            slots("xz", 0, bc(3))
            slots("xz", 1, during_z(0))
            with act.Fori(1, SG) as g:
                slots("xz", g * 2, during_xs(g - 1))
                slots("xz", g * 2 + 1, join({0: [lambda: y_scale(g - 1)], 1: [lambda: ssd_hi(g - 1)]}, during_z(g)))
            slots("sig_b", 0, during_xs(SG - 1))

            def sig_b_first():
                act.wait_ge(tp_done, PACKS["xz"] + 48)
                sig_to("sig_b", 0, sig_b)

            slots("sig_b", 1, {0: [lambda: y_scale(SG - 1)], 1: [lambda: ssd_hi(SG - 1)], 4: [sig_b_first]})
            with act.Fori(2, 4) as i:
                slots("sig_b", i, {1: [lambda: sig_to("sig_b", i - 1, sig_b)]})

            def merge_hi(i):
                for j in range(2):
                    hi_pack("ssd_out", 2 * i + j, j, 4 * i + (AT_X + 2 * j))

            slots("ssd_out", 0, {1: [lambda: sig_to("sig_b", 3, sig_b)]})
            with act.Fori(1, 4) as i:
                slots("ssd_out", i, {5: [lambda: merge_hi(i - 1)]})

            def mem_squares():
                act.drain()
                for s in in_mem:
                    act.wait_ge(s, 16)
                for t in range(NT):
                    for j in range(4):
                        act.activation(junk[:, :], mem_n[:, t, j * N:(j + 1) * N], ACT.Square,
                                       accum_out=ss_ff4[:, t * 4 + j:t * 4 + j + 1])
                        act.drain()
                act.nop().then_inc(ss_done, 1)

            def mem_hi(lo, hi):
                for m in range(lo, hi):
                    hi_pack("mem", m, m % 2, AT_MEM + 2 * m, V_MEM + 2 * m)

            def h_save(base, i, ss4):
                act.wait_ge(hg_ready, base + i + 1)
                o = hres[:, :, i * N:(i + 1) * N] if isinstance(i, int) else hres[:, :, ds(i * N, N)]
                copy(o, nat[:, :, :])
                for t in range(NT):
                    a = ss4[:, 2 * i + t:2 * i + t + 1] if isinstance(i, int) else ss4[:, ds(i * 2 + t, 1)]
                    last = act.activation(junk[:, :], nat[:, t, :], ACT.Square, accum_out=a)
                    act.drain() if t == 0 else None
                last.then_inc(h_saved, 1)

            def h_hi(phase, i, at, col):
                for j in range(2):
                    hi_pack(phase, 2 * i + j, j, 4 * i + (at + 2 * j), 4 * i + (col + 2 * j))

            def mix(i):
                return {0: [lambda: h_save(0, i, ss_xa4)], 2: [lambda: h_hi("mix", i, AT_XA, V_XA)]}

            slots("mix", 0, {3: [lambda: merge_hi(3)], 5: [lambda: mem_hi(0, 2)], 6: [lambda: mem_hi(2, 4)],
                             7: [lambda: mem_hi(4, 6)]})
            slots("mix", 1, join({0: [lambda: mem_hi(6, 8)]}, mix(0), {4: [mem_squares], 6: [lambda: root(3, rs_mem)]}))
            with act.Fori(2, 4) as i:
                slots("mix", i, mix(i - 1))

            def v_copy(i):
                group_ready("xv", i)
                for t in range(NT):
                    o = v_x[:, t, i * N:(i + 1) * N] if isinstance(i, int) else v_x[:, t, ds(i * N, N)]
                    last = copy(o, acc_of(i, t), rs_mem[:, t:t + 1])
                last.then_inc(acc_read, 1)

            def v_first():
                act.wait_ge(merged_ready, 4)
                act.wait_ge(rs_done, 3)
                v_copy(0)

            slots("xv", 0, {**mix(3), 5: [lambda: root(4, rs_xa)]})
            slots("xv", 1, {1: [v_first]})
            with act.Fori(2, 4) as i:
                slots("xv", i, {1: [lambda: v_copy(i - 1)]})

            def k_copy(n):
                m = PACKS["mix"] + 8 if isinstance(n, int) and n == 0 else n * 6 + (PACKS["kq"] - 2)
                nat_copy("kq", 2 * n, m, rs_mem, parity=0)

            def turned(m, n, dst):
                for j in range(2):
                    act.wait_ge(tp_done, PACKS["kq"] + 6 * n + m + j + 1)
                    copy(dst[:, 2 * j:2 * j + 2, :], ptr[:, j, :].rearrange("p (k n) -> p k n", k=2)) \
                        .then_inc(tp_read, 1)

            def k_turned(n):
                need(act, xscores_done, n)
                turned(0, n, kx_t)

            def q_copy(n):
                nat_copy("kq", 2 * n + 1, PACKS["kq"] + 6 * n + 2, rs_xa, parity=1)

            def q_turned(n):
                turned(2, n, qx_t)

            def softmax_exp(n):
                act.wait_ge(nmx_ready, n + 1)
                need(act, pt_done, n)
                for t in range(NT):
                    last = act.activation(prob[:, t, :], pss[:, 0, t * T:(t + 1) * T], ACT.Exp,
                                          bias=nmx[:, t:t + 1], scale=XD ** -0.5, accum_out=sm[:, t:t + 1])
                last.then_inc(prob_ready, 1)

            def p_copy(n):
                act.wait_ge(pt_done, n + 1)
                copy(prob_t, pss[:, 1, :]).then_inc(pt_copied, 1)

            def o_hi(n):
                for j in range(2):
                    hi_pack("kq", 6 * n + 4 + j, j, 4 * n + (AT_X + 2 * j))

            def attention(n):
                return {0: [lambda: q_copy(n)], 1: [lambda: q_turned(n)], 2: [lambda: softmax_exp(n)],
                        3: [lambda: p_copy(n)], 5: [lambda: o_hi(n)]}

            slots("kq", 0, {1: [lambda: v_copy(3)]})
            slots("kq", 1, {1: [lambda: k_copy(0)], 2: [lambda: k_turned(0)]})
            with act.Fori(1, XH) as n:
                slots("kq", n * 2, attention(n - 1))
                slots("kq", n * 2 + 1, {1: [lambda: k_copy(n)], 2: [lambda: k_turned(n)]})

            def xo(i):
                return {0: [lambda: h_save(4, i, ss_ff4)], 2: [lambda: h_hi("xo", i, AT_FF, V_FF)]}

            slots("xo", 0, attention(XH - 1))
            with act.Fori(1, 4) as i:
                slots("xo", i, xo(i - 1))

            def relu(phase, i):
                group_ready(phase, i)
                need(act, sq_ready, (8 if phase == "ff1b" else 0) + i)
                for t in range(NT):
                    last = act.activation(nat[:, t, :], acc_of(i, t), ACT.Relu, scale=rs_ff[:, t:t + 1])
                last.then_inc(acc_read, 1)

            def sq_hi(phase, i):
                for j in range(2):
                    hi_pack(phase, 2 * i + j, j, 4 * i + (AT_HID + 2 * j))

            def relu_first():
                act.wait_ge(rs_done, 5)
                relu("ff1a", 0)

            def up(phase, i):
                return {0: [lambda: relu(phase, i)], 2: [lambda: sq_hi(phase, i)]}

            slots("ff1a", 0, {**xo(3), 5: [lambda: root(5, rs_ff)]})
            slots("ff1a", 1, {0: [relu_first], 2: [lambda: sq_hi("ff1a", 0)]})
            with act.Fori(2, 8) as i:
                slots("ff1a", i, up("ff1a", i - 1))
            slots("ff2a", 0, up("ff1a", 7))
            with act.Fori(1, 4) as i:
                slots("ff2a", i, {})
            slots("ff1b", 0, {})
            with act.Fori(1, 8) as i:
                slots("ff1b", i, up("ff1b", i - 1))
            slots("ff2b", 0, up("ff1b", 7))
            def out_squares(i):
                act.drain()
                for t in range(NT):
                    if isinstance(i, int):
                        act.wait_ge(out_added, 2 * i + t + 1)
                        h, a = hres[:, t, i * N:(i + 1) * N], ss_out4[:, 2 * i + t:2 * i + t + 1]
                    else:
                        act.wait_ge(out_added, i * 2 + (t + 1))
                        h, a = hres[:, t, ds(i * N, N)], ss_out4[:, ds(i * 2 + t, 1)]
                    last = act.activation(nat[:, t, :], h, ACT.Square, accum_out=a)
                last.then_inc(out_squared, 1)

            with act.Fori(1, 3) as i:
                slots("ff2b", i, {2: [lambda: out_squares(i - 1)]})
            slots("ff2b", 3, {2: [lambda: out_squares(2)]}, final=True)

            out_squares(3)
            root(6, rs_out)
            act.wait_ge(rs_done, 6)
            act.wait_ge(out_gained, 3)
            for t in range(NT):
                h = hres[:, t, 0:D // 2]
                copy(h, h, rs_out[:, t:t + 1]).then_inc(fin_act, 1)

        @block.vector
        def _(dve):
            def tt(o, a, b, op):
                return dve.tensor_tensor(o, a, b, op)

            def split_lo(phase, i, c):
                n = CHUNK[phase] + CPG[phase] * i + c + LEAD
                s = (c + LEAD) % RAW
                dve.wait_ge(hi_ready, n + 1)
                tt(w_lo[:, s, :], raw[:, s, :], w_hi[:, s, :].bitcast(F32), ALU.subtract).then_inc(lo_ready, 1)

            def slots(phase, i, hooks, final=False):
                for c in range(CPG[phase]):
                    if not (final and c + LEAD >= CPG[phase]):
                        split_lo(phase, i, c)
                    if c in hooks:
                        dve.drain()
                    for step in hooks.get(c, ()):
                        step()

            def group_ready(phase, i):
                dve.wait_ge(w_used, group_end(phase, i))
                need(dve, acc_read, GROUP[phase] + i)

            def lo_pack(split, m, b, at, col=None):
                dve.wait_ge(tp_hi, SPLITS[split] + m + 1)
                if col is None:
                    a = slice(at, at + 2) if isinstance(at, int) else ds(at, 2)
                    tt(acts_lo[:, a, :], ptr[:, b, :].rearrange("p (k n) -> p k n", k=2),
                       acts_hi[:, a, :].bitcast(F32), ALU.subtract).then_inc(tp_read, 1)
                    return
                for k in range(2):
                    a, v = at + k, col + k
                    if isinstance(a, int):
                        lo, hi = acts_lo[:, a, :], acts_hi[:, a, :]
                    else:
                        lo = acts_lo[:, ds(a, 1), :].rearrange("p a n -> p (a n)")
                        hi = acts_hi[:, ds(a, 1), :].rearrange("p a n -> p (a n)")
                    sc = vec[:, v:v + 1] if isinstance(v, int) else vec[:, ds(v, 1)]
                    last = dve.scalar_tensor_tensor(lo, ptr[:, b, k * T:(k + 1) * T], sc, hi.bitcast(F32),
                                                    ALU.mult, ALU.subtract)
                last.then_inc(tp_read, 1)

            def mean_square(ss, out_, width):
                return dve.tensor_scalar(out_, ss, 1.0 / width, EPS, ALU.mult, ALU.add)

            def rstd(n, v):
                dve.wait_ge(sqrt_done, n)
                dve.reciprocal(v, v).then_inc(rs_done, 1)
                dve.drain()

            dve.wait_ge(vec_turned, 1)
            dve.tensor_copy(vec[:, 0:KT], pss[:, 0, 0:KT]).then_inc(vec_ready, 1)
            dve.drain()

            def x_lo(m):
                lo_pack("x", m, m % 2, AT_X + 2 * m, V_MIX + 2 * m)

            for n in range(LEAD):
                dve.wait_ge(hi_ready, n + 1)
                tt(w_lo[:, n, :], raw[:, n, :], w_hi[:, n, :].bitcast(F32), ALU.subtract).then_inc(lo_ready, 1)
                if n < 2:
                    x_lo(n)

            def vec_copy():
                dve.wait_ge(vec_turned, 2)
                dve.tensor_copy(vec[:, KT:], pss[:, 0, KT:V_ALL]).then_inc(vec_ready, 1)

            def x_var():
                dve.wait_ge(ss_done, NT)
                mean_square(ss_x, rs_x, D).then_inc(var_done, 1)

            def rotate(i):
                dve.wait_ge(acc_read, GROUP["qkv"] + i + 1)
                need(dve, qk_turned, i)
                need(dve, scores_done, i)
                qk = qkv[:, :, 0:2 * DK].rearrange("p t (a d) -> p t a d", a=4)
                tt(rot_a, qk, cos.broadcast_to([P, NT, 4, DK // 2]), ALU.mult)
                tt(rot_b, qk, sin.broadcast_to([P, NT, 4, DK // 2]), ALU.mult)
                dve.drain()
                a2 = rot_a.rearrange("p t (a h) d -> p (t a) h d", h=2)
                b2 = rot_b.rearrange("p t (a h) d -> p (t a) h d", h=2)
                r2 = rot.rearrange("p t (a h) d -> p (t a) h d", h=2)
                tt(r2[:, :, 0, :], a2[:, :, 0, :], b2[:, :, 1, :], ALU.subtract)
                tt(r2[:, :, 1, :], a2[:, :, 1, :], b2[:, :, 0, :], ALU.add).then_inc(rotated, 1)
                dve.drain()
                z = cst[:, C_ZETA + i:C_ZETA + i + 1] if isinstance(i, int) else cst[:, ds(i + C_ZETA, 1)]
                dve.tensor_scalar(k_z, rotm[:, 0, 1, :], z, None, ALU.mult).then_inc(kz_ready, 1)

            def decay_scores(i):
                dve.wait_ge(scores_done, i + 1)
                need(dve, inner_done, i)
                d = dec_t[:, i:i + 1, :] if isinstance(i, int) else dec_t[:, ds(i, 1), :]
                tt(s_t, pss[:, 1, 0:T].rearrange("p (c n) -> p c n", c=NT), d.broadcast_to([P, NT, P]), ALU.mult) \
                    .then_inc(decayed, 1)

            def ret_y(i):
                dve.wait_ge(inner_done, i + 1)
                cols = slice(i * DV, (i + 1) * DV) if isinstance(i, int) else ds(i * DV, DV)
                dve.tensor_copy(y_ret[:, 0, cols], ptr[:, 0, 0:DV])
                dve.wait_ge(cross_copied, i + 1)
                tt(y_ret[:, 1, cols], ptr[:, 0, DV:2 * DV], cross_sb, ALU.add)
                dve.drain()
                for t in range(NT):
                    dve.bn_stats(bnst[:, t, :], y_ret[:, t, cols])
                dve.drain()
                for t in range(NT):
                    dve.bn_aggr(bnag[:, 2 * t:2 * t + 2], bnst[:, t, :])
                dve.drain()
                m = mv[:, 4 * i:4 * i + 4] if isinstance(i, int) else mv[:, ds(i * 4, 4)]
                dve.tensor_copy(m, bnag).then_inc(y_stored, 1)
                dve.drain()

            def retention(i):
                return {0: [lambda: rotate(i)], 4: [lambda: decay_scores(i)], 6: [lambda: ret_y(i)]}

            slots("qkv", 0, {0: [lambda: x_lo(2), lambda: x_lo(3)],
                             **{c: [lambda m=c + 2: x_lo(m)] for c in range(2, 6)},
                             6: [vec_copy, x_var], 7: [ lambda: rstd(1, rs_x), lambda: dve.wait_ge(in_dec, 16)]})
            with dve.Fori(1, HEADS) as i:
                slots("qkv", i, retention(i - 1))

            def head_vars():
                v = mv.rearrange("p (j s) -> p j s", s=2)[:, :, 1]
                dve.tensor_scalar(rgn, v, EPS, None, ALU.add).then_inc(var_done, 1)

            def gate_mul(i):
                for t in range(NT):
                    for h in range(2):
                        if isinstance(i, int):
                            y = y_ret[:, t, i * N + h * DV:i * N + (h + 1) * DV]
                            j = 4 * i + 2 * h + t
                            mu, r = mv[:, 2 * j:2 * j + 1], rgn[:, j:j + 1]
                        else:
                            y = y_ret[:, t, ds(i * N + h * DV, DV)]
                            mu, r = mv[:, ds(i * 8 + (4 * h + 2 * t), 1)], rgn[:, ds(i * 4 + (2 * h + t), 1)]
                        dve.tensor_scalar(y, y, mu, r, ALU.subtract, ALU.mult)
                dve.drain()
                dve.wait_ge(acc_read, GROUP["gate"] + i + 1)
                cols = slice(i * N, (i + 1) * N) if isinstance(i, int) else ds(i * N, N)
                tt(gated, y_ret[:, :, cols], gated, ALU.mult).then_inc(gated_ready, 1)

            def gate_lo(i):
                for j in range(2):
                    lo_pack("gate", 2 * i + j, j, 4 * i + (AT_RET + 2 * j), 4 * i + (V_RET + 2 * j))

            def gate(i):
                return {0: [lambda: gate_mul(i)], 3: [lambda: gate_lo(i)]}

            slots("gate", 0, join(retention(HEADS - 1), {6: [head_vars], 7: [lambda: rstd(2, rgn)]}))
            with dve.Fori(1, 4) as i:
                slots("gate", i, gate(i - 1))
            slots("sig_a", 0, gate(3))
            with dve.Fori(1, 4) as i:
                slots("sig_a", i, {})

            def branch_a(i):
                group_ready("ret_out", i)
                cols = slice(i * N, (i + 1) * N) if isinstance(i, int) else ds(i * N, N)
                tt(merged[:, :, cols], acc_both(i), sig_a[:, :, cols], ALU.mult).then_inc(acc_read, 1)

            slots("ret_out", 0, {})
            with dve.Fori(1, 4) as i:
                slots("ret_out", i, {1: [lambda: branch_a(i - 1)]})
            slots("dt", 0, {1: [lambda: branch_a(3)]})

            wk = junk[:, :].rearrange("p (a t n) -> p a t n", a=4, t=NT)

            def dt_in():
                dve.wait_ge(dt_turned, 1)
                dve.wait_ge(in_head, 48)
                for t in range(NT):
                    dve.scalar_tensor_tensor(wk[:, 0, t], pss[:, 1, t * SH:(t + 1) * SH], rs_x[:, t:t + 1],
                                             headrow[:, 0, :], ALU.mult, ALU.add)
                dve.drain()
                dve.scalar_tensor_tensor(wk[:, 1], wk[:, 0], -1.0, wk[:, 0], ALU.mult, ALU.min) \
                    .then_inc(neg_abs_ready, 1)

            def dt_w():
                dve.wait_ge(exps_ready, 2)
                dve.tensor_scalar(wk[:, 2], wk[:, 1], 1.0, None, ALU.add).then_inc(one_plus_ready, 1)

            def dt_out():
                dve.wait_ge(ln_ready, 1)
                dve.tensor_scalar(wk[:, 2], wk[:, 2], 1.0, None, ALU.subtract)
                dve.drain()
                dve.tensor_scalar(da[:, :, :], wk[:, 2], 0.0, None, ALU.is_equal)
                dve.drain()
                tt(wk[:, 2], wk[:, 2], da[:, :, :], ALU.add)
                tt(da[:, :, :], da[:, :, :], wk[:, 1], ALU.mult)
                dve.drain()
                dve.reciprocal(wk[:, 2], wk[:, 2])
                tt(wk[:, 3], wk[:, 3], wk[:, 1], ALU.mult)
                dve.drain()
                tt(wk[:, 3], wk[:, 3], wk[:, 2], ALU.mult)
                dve.drain()
                tt(wk[:, 3], wk[:, 3], da[:, :, :], ALU.add)
                dve.drain()
                dve.scalar_tensor_tensor(dtt[:, :, :], wk[:, 0], 0.0, wk[:, 3], ALU.max, ALU.add)
                dve.drain()
                for t in range(NT):
                    last = dve.scalar_tensor_tensor(da[:, t, :], dtt[:, t, :], -1.0, headrow[:, 1, :],
                                                    ALU.mult, ALU.mult)
                last.then_inc(da_ready, 1)

            def to_end():
                dve.wait_ge(acs_copied, 1)
                tt(dstate[:, :], junk[:, 0:SH], nacs[:, 0, :], ALU.add).then_inc(ds_ready, 1)

            def conv_pack(b, q0, ct):
                def col(v, k):
                    v = ct + (v + k)
                    return vec[:, v:v + 1] if isinstance(v, int) else vec[:, ds(v, 1)]
                for j in range(2, -1, -1):
                    back = 3 - j
                    for k in range(2):
                        src, o = ptr[:, b, k * T:(k + 1) * T], conv[:, q0 + k, :]
                        last = dve.scalar_tensor_tensor(o[:, back:], src[:, 0:T - back],
                                                        col(V_CW + j * (CONV // P), k), o[:, back:],
                                                        ALU.mult, ALU.add)
                    if j:
                        dve.drain()
                return last

            def bc_conv(i):
                for j in range(2):
                    dve.wait_ge(tap_done, 2 * i + j + 1)
                    conv_pack(j, 2 * j, i * 4 + (INNER // P + 2 * j)).then_inc(tp_read, 1)
                dve.drain()
                dve.nop().then_inc(conv_done, 1)

            slots("bc", 0, {1: [dt_in], 2: [dt_w], 5: [dt_out]})
            slots("bc", 1, {1: [to_end], 4: [lambda: bc_conv(0)]})
            with dve.Fori(2, 4) as i:
                slots("bc", i, {4: [lambda: bc_conv(i - 1)]})

            def by_head(ap, g, cnt):
                a = ap[:, g * RH:(g + 1) * RH] if isinstance(g, int) else ap[:, ds(g * RH, RH)]
                return a.rearrange("p (r a) -> p r a", a=1).broadcast_to([P, RH, cnt])

            def xs_conv(g, j):
                dve.wait_ge(tap_done, 8 + 2 * g + j + 1)
                conv_pack(j, 2 * j, g * 4 + 2 * j).then_inc(tp_read, 1)
                dve.drain()
                dve.nop().then_inc(xconv_done, 1)

            def heads3(ap):
                return ap.rearrange("p (r d) -> p r d", r=RH)

            def xdt_mul(g):
                dve.wait_ge(tp_read, PACKS["xz"] + 6 * g + 4)
                need(dve, ydiag_done, 2 * g)
                for t in range(NT):
                    tt(heads3(xdt[:, t, :]), heads3(xs_n[:, t, :]), by_head(dtt[:, t, :], g, SP_), ALU.mult)
                need(dve, tp_done, PACKS["xz"] + 6 * g)
                for t in range(NT):
                    tt(heads3(y_ssd[:, t, :]), heads3(xs_n[:, t, :]), by_head(headrow[:, 2, :], g, SP_), ALU.mult)
                dve.drain()
                tt(heads3(xdtd), heads3(xdt[:, 0, :]), by_head(dstate[:, :], g, SP_), ALU.mult) \
                    .then_inc(xdt_ready, 1)

            def seg_max(g, c):
                dve.wait_ge(in_nacs, (g + 1) * 16)
                e3 = heads3(e_m[c])
                tt(e3, e3, by_head(nacs[:, c, :], g, P), ALU.max).then_inc(seg_ready, 1)

            def mask_cb(g):
                dve.wait_ge(cb_done, g + 1)
                dve.wait_ge(cross_ready, g + 1)
                tt(cbm, ptr[:, 0, :].rearrange("p (c l) -> p c l", c=NT)[:, :, 0:P],
                   tri.rearrange("p (a l) -> p a l", a=1).broadcast_to([P, NT, P]), ALU.mult)

            def decay_cb(g, c):
                dve.wait_ge(exp_done, 2 * g + c + 1)
                e3 = e_m[c].rearrange("p (r l) -> p r l", r=RH)
                tt(e3, e3, cbm[:, c:c + 1, :].broadcast_to([P, RH, P]), ALU.mult).then_inc(mt_ready, 1)

            def add_y0(g):
                dve.wait_ge(ydiag_done, 2 * g + 1)
                tt(y_ssd[:, 0, :], pss[:, 0, :], y_ssd[:, 0, :], ALU.add).then_inc(y_added, 1)

            def add_off(g):
                dve.wait_ge(yoff_done, g + 1)
                tt(heads3(junk[:, :]), heads3(ptr[:, 1, :]), by_head(eacs[:, :], g, SP_), ALU.mult)
                dve.drain()
                tt(y_ssd[:, 1, :], junk[:, :], y_ssd[:, 1, :], ALU.add).then_inc(y_added, 1)

            def add_y1(g):
                dve.drain()
                dve.wait_ge(ydiag_done, 2 * g + 2)
                tt(y_ssd[:, 1, :], pss[:, 1, :], y_ssd[:, 1, :], ALU.add).then_inc(y_added, 1)
                dve.drain()
                dve.wait_ge(acc_read, GROUP["xz"] + 2 * g + 2)
                tt(y_ssd, y_ssd, s_z, ALU.mult).then_inc(y_gated, 1)

            def y_var(g):
                dve.wait_ge(gss_done, g + 1)
                mean_square(ss_g, rs_g, N).then_inc(gvar_done, 1)

            def y_rstd(g):
                dve.wait_ge(gsqrt_done, g + 1)
                dve.reciprocal(rs_g, rs_g).then_inc(grs_done, 1)

            def ssd_lo(g):
                for j in range(2):
                    lo_pack("xz", 2 * g + j, j, 4 * g + (AT_SSD + 2 * j), 4 * g + (V_SSD + 2 * j))

            def during_z(g):
                return {3: [lambda: xs_conv(g, 0)], 4: [lambda: xs_conv(g, 1)], 6: [lambda: seg_max(g, 0)],
                        7: [lambda: xdt_mul(g)]}

            def during_xs(g):
                return {0: [lambda: seg_max(g, 1)], 1: [lambda: mask_cb(g)], 2: [lambda: decay_cb(g, 0)],
                        3: [lambda: decay_cb(g, 1)], 4: [lambda: add_y0(g), lambda: add_off(g)],
                        5: [lambda: add_y1(g)], 6: [lambda: y_var(g)], 7: [lambda: y_rstd(g)]}

            def before_ssd():
                dve.wait_ge(ds_exp, 1)
                dve.wait_ge(m_stored, 16)

            slots("xz", 0, {4: [lambda: bc_conv(3), before_ssd]})
            slots("xz", 1, during_z(0))
            with dve.Fori(1, SG) as g:
                slots("xz", g * 2, during_xs(g - 1))
                slots("xz", g * 2 + 1, join({1: [lambda: ssd_lo(g - 1)]}, during_z(g)))
            slots("sig_b", 0, during_xs(SG - 1))
            slots("sig_b", 1, {1: [lambda: ssd_lo(SG - 1)]})
            with dve.Fori(2, 4) as i:
                slots("sig_b", i, {})

            def merge(i):
                group_ready("ssd_out", i)
                cols = slice(i * N, (i + 1) * N) if isinstance(i, int) else ds(i * N, N)
                tt(sig_b[:, :, cols], acc_both(i), sig_b[:, :, cols], ALU.mult).then_inc(acc_read, 1)
                dve.drain()
                need(dve, tp_done, PACKS["ssd_out"] + 2 * i)
                tt(nat[:, :, :], sig_b[:, :, cols], merged[:, :, cols], ALU.add).then_inc(merged_ready, 1)

            def merge_lo(i):
                for j in range(2):
                    lo_pack("ssd_out", 2 * i + j, j, 4 * i + (AT_X + 2 * j))

            slots("ssd_out", 0, {5: [lambda: dve.wait_ge(in_m, 16)]})
            with dve.Fori(1, 4) as i:
                slots("ssd_out", i, {1: [lambda: merge(i - 1)], 5: [lambda: merge_lo(i - 1)]})

            def mem_lo(lo, hi):
                for m in range(lo, hi):
                    lo_pack("mem", m, m % 2, AT_MEM + 2 * m, V_MEM + 2 * m)

            def sum4(ss4, pattern, out_, width):
                dve.tensor_reduce(out_, ss4.rearrange(pattern, t=NT), axis=AX.X, op=ALU.add)
                dve.drain()
                mean_square(out_, out_, width).then_inc(var_done, 1)

            def mem_var():
                dve.wait_ge(ss_done, NT + 1)
                sum4(ss_ff4, "p (t j) -> p t j", rs_mem, D)

            def h_add(phase, base, i, m):
                group_ready(phase, i)
                need(dve, tp_done, m)
                need(dve, h_saved, base + i)
                cols = slice(i * N, (i + 1) * N) if isinstance(i, int) else ds(i * N, N)
                tt(nat[:, :, :], acc_both(i), hres[:, :, cols], ALU.add).then_inc(acc_read, 1)

            def h_lo(phase, i, at, col):
                for j in range(2):
                    lo_pack(phase, 2 * i + j, j, 4 * i + (at + 2 * j), 4 * i + (col + 2 * j))

            def mix_add(i):
                first = isinstance(i, int) and i == 0
                h_add("mix", 0, i, PACKS["ssd_out"] + 8 if first else PACKS["mix"] + 2 * i)
                dve.drain()
                dve.nop().then_inc(hg_ready, 1)

            slots("mix", 0, {1: [lambda: merge(3)], 3: [lambda: merge_lo(3)], 5: [lambda: mem_lo(0, 2)],
                             6: [lambda: mem_lo(2, 4)], 7: [lambda: mem_lo(4, 6)]})

            def mix(i):
                return {0: [lambda: mix_add(i)], 2: [lambda: h_lo("mix", i, AT_XA, V_XA)]}

            slots("mix", 1, join({0: [lambda: mem_lo(6, 8), lambda: dve.wait_ge(in_h, 16)]}, mix(0),
                                 {5: [mem_var], 7: [lambda: rstd(3, rs_mem)]}))
            with dve.Fori(2, 4) as i:
                slots("mix", i, mix(i - 1))

            def xa_var():
                dve.wait_ge(h_saved, 4)
                sum4(ss_xa4, "p (j t) -> p t j", rs_xa, D)

            slots("xv", 0, {**mix(3), 4: [xa_var], 6: [lambda: rstd(4, rs_xa)]})
            with dve.Fori(1, 4) as i:
                slots("xv", i, {})

            def softmax_max(n):
                dve.wait_ge(xscores_done, n + 1)
                dve.reduce_max(mx, pss[:, 0, :].rearrange("p (t m) -> p t m", t=NT), AX.X)
                dve.drain()
                dve.tensor_scalar(nmx, mx, -(XD ** -0.5), None, ALU.mult).then_inc(nmx_ready, 1)

            def o_scale(n):
                dve.wait_ge(prob_ready, n + 1)
                dve.reciprocal(rsm, sm)
                dve.drain()
                dve.wait_ge(pv_done, n + 1)
                need(dve, tp_done, PACKS["kq"] + 6 * n)
                for t in range(NT):
                    last = dve.tensor_scalar(o_n[:, t, :], pss[:, t, :], rsm[:, t:t + 1], None, ALU.mult)
                last.then_inc(o_ready, 1)

            def o_lo(n):
                for j in range(2):
                    lo_pack("kq", 2 * n + j, j, 4 * n + (AT_X + 2 * j))

            def attention(n):
                return {1: [lambda: softmax_max(n)], 3: [lambda: o_scale(n)], 5: [lambda: o_lo(n)]}

            slots("kq", 0, {})
            slots("kq", 1, {})
            with dve.Fori(1, XH) as n:
                slots("kq", n * 2, attention(n - 1))
                slots("kq", n * 2 + 1, {})
            slots("xo", 0, attention(XH - 1))

            def xo_add(i):
                first = isinstance(i, int) and i == 0
                h_add("xo", 4, i, PACKS["kq"] + 24 if first else PACKS["xo"] + 2 * i)
                dve.drain()
                dve.nop().then_inc(hg_ready, 1)

            def xo(i):
                return {0: [lambda: xo_add(i)], 2: [lambda: h_lo("xo", i, AT_FF, V_FF)]}

            with dve.Fori(1, 4) as i:
                slots("xo", i, xo(i - 1))

            def ff_var():
                dve.wait_ge(h_saved, 8)
                sum4(ss_ff4, "p (j t) -> p t j", rs_ff, D)

            def square(phase, i):
                dve.wait_ge(acc_read, GROUP[phase] + i + 1)
                need(dve, tp_done, (PACKS["xo"] + 8 if isinstance(i, int) and i == 0 and phase == "ff1a"
                                    else PACKS[phase] + 2 * i))
                tt(sq_n, nat[:, :, :], nat[:, :, :], ALU.mult).then_inc(sq_ready, 1)

            def sq_lo(phase, i):
                for j in range(2):
                    lo_pack(phase, 2 * i + j, j, 4 * i + (AT_HID + 2 * j))

            def up(phase, i):
                return {0: [lambda: square(phase, i)], 2: [lambda: sq_lo(phase, i)]}

            def down_add(phase, i):
                group_ready(phase, i)
                cols = slice(i * N, (i + 1) * N) if isinstance(i, int) else ds(i * N, N)
                tt(hres[:, :, cols], acc_both(i), hres[:, :, cols], ALU.add).then_inc(acc_read, 1)

            slots("ff1a", 0, {**xo(3), 4: [ff_var], 6: [lambda: rstd(5, rs_ff)]})
            with dve.Fori(1, 8) as i:
                slots("ff1a", i, up("ff1a", i - 1))
            slots("ff2a", 0, up("ff1a", 7))
            with dve.Fori(1, 4) as i:
                slots("ff2a", i, {1: [lambda: down_add("ff2a", i - 1)]})
            slots("ff1b", 0, {1: [lambda: down_add("ff2a", 3)]})
            with dve.Fori(1, 8) as i:
                slots("ff1b", i, up("ff1b", i - 1))
            slots("ff2b", 0, join(up("ff1b", 7), {5: [lambda: dve.wait_ge(in_fn, 16)]}))

            def last_add(i):
                group_ready("ff2b", i)
                for t in range(NT):
                    h = hres[:, t, i * N:(i + 1) * N] if isinstance(i, int) else hres[:, t, ds(i * N, N)]
                    last = tt(h, acc_of(i, t), h, ALU.add).then_inc(out_added, 1)
                dve.drain()
                dve.nop().then_inc(acc_read, 1)

            def gain(i):
                dve.wait_ge(out_squared, i + 1)
                cols = slice(i * N, (i + 1) * N) if isinstance(i, int) else ds(i * N, N)
                h, f = hres[:, :, cols], fnw[:, cols].rearrange("p (a n) -> p a n", a=1)
                tt(h, h, f.broadcast_to([P, NT, N]), ALU.mult).then_inc(out_gained, 1)

            with dve.Fori(1, 3) as i:
                slots("ff2b", i, {1: [lambda: last_add(i - 1)], 5: [lambda: gain(i - 1)]})
            slots("ff2b", 3, {1: [lambda: last_add(2)], 5: [lambda: gain(2)]}, final=True)
            last_add(3)

            dve.wait_ge(out_squared, 4)
            sum4(ss_out4, "p (j t) -> p t j", rs_out, D)
            rstd(6, rs_out)
            for t in range(NT):
                h = hres[:, t, 2 * N:3 * N]
                dve.tensor_scalar(h, h, rs_out[:, t:t + 1], None, ALU.mult)
                h = hres[:, t, 3 * N:]
                dve.scalar_tensor_tensor(h, h, rs_out[:, t:t + 1], fnw[:, 3 * N:], ALU.mult, ALU.mult) \
                    .then_inc(fin_dve, 1)


def constants():
    f = np.float32
    c = np.zeros((P, C_ALL), f)
    i = np.arange(P)
    c[:, C_ID:C_ID + P] = np.eye(P, dtype=f)
    c[:, C_TRI:C_TRI + P] = i[:, None] <= i[None, :]
    c[:, C_ONE:C_ONE + P] = 1.0
    half = DK // 2
    inv = np.exp(f(-math.log(10000.0)) * np.arange(half, dtype=f) / f(half)).astype(f)
    ang = (np.arange(T, dtype=f)[:, None] * inv[None, :]).astype(f)
    for at, fn in ((C_COS, np.cos), (C_SIN, np.sin)):
        c[:, at:at + P] = fn(ang.astype(np.float64)).astype(f).reshape(NT, P, half).transpose(1, 0, 2).reshape(P, P)
    log_g = np.log(f(1.0) - np.exp2(f(-5.0) - np.arange(HEADS, dtype=f))).astype(f)
    idx = np.arange(P, dtype=f)
    c[:, C_ZETA:C_ZETA + HEADS] = np.exp((f(P - 1) - idx)[:, None] * log_g[None, :])
    c[:, C_XI:C_XI + HEADS] = np.exp((idx + f(1))[:, None] * log_g[None, :])
    rel = idx[None, :] - idx[:, None]
    dec = np.where(rel[:, None, :] >= 0, np.exp(np.maximum(rel, 0)[:, None, :] * log_g[None, :, None]), 0)
    return c, dec.astype(f).reshape(P, HEADS * P)


_INS = ['x', 'mem', 'w_in', 'conv_w', 'conv_b', 'dt_bias', 'a_log', 'd_skip', 'norm_mix_w', 'ret_norm_w',
        'ssd_norm_w', 'w_ret_out', 'w_ssd_out', 'w_mix_out', 'norm_xa_w', 'mem_norm_w', 'w_xq', 'w_xkv', 'w_xo',
        'norm_ff_w', 'w_ff1', 'w_ff2', 'final_norm_w']


def kernel(**inputs):
    import concourse.bacc as _bacc
    from concourse.bass_utils import run_bass_kernel_spmd as _run

    nc = _bacc.Bacc("TRN2", target_bir_lowering=False, num_devices=1)
    arrays, args = {}, {}

    def give(name, a):
        arrays[f"in_{name}"] = a
        args[name] = nc.dram_tensor(f"in_{name}", a.shape, mybir.dt.from_np(a.dtype), kind="ExternalInput").ap()

    for name in _INS:
        give(name, np.ascontiguousarray(inputs[name]))
    cst, dec = constants()
    give("consts", cst)
    give("decay", dec)
    args["merged_dram"] = nc.dram_tensor("merged_dram", (P, NT * D), F32, kind="Internal").ap()
    args["nacs_dram"] = nc.dram_tensor("nacs_dram", (NT, SH * P), F32, kind="Internal").ap()
    args["out"] = nc.dram_tensor("out_0", (1, T, D), F32, kind="ExternalOutput").ap()
    hybrid_layer(nc, **args)
    r = _run(nc, [arrays], core_ids=[0])
    return r.results[0]["out_0"]
```
